# Optimizing a Trainium2 kernel written in Bass

```python
import math
import jax, jax.numpy as jnp
from jax import lax
import numpy as np

D_MODEL = 1024
BATCH = 1
SEQ = 512
DEPTH = 2

CHUNK = 64
N_MIXERS = 2

SG_FFN = 6 * D_MODEL
SG_WIDTH = SG_FFN // 2
SG_BLOCK = 128
SG_GROUPS = 8
SG_GC = SG_WIDTH // SG_GROUPS

GLA_HEADS = 4
GLA_KD = D_MODEL // 2
GLA_VD = D_MODEL
GLA_DK = GLA_KD // GLA_HEADS
GLA_DV = GLA_VD // GLA_HEADS
GLA_RANK = 16
GLA_TAU = 16.0
GLA_IN = 2 * GLA_KD + 2 * GLA_VD + GLA_RANK

FFN_HIDDEN = ((8 * D_MODEL + 3 * 256 - 1) // (3 * 256)) * 256

EPS = 1e-6

kernel_name = "hybrid_gmlp_gla_chunk_causal_trunk"

def rmsnorm(x, g):
    xf = x.astype(jnp.float32)
    y = xf * lax.rsqrt(jnp.mean(xf * xf, axis=-1, keepdims=True) + EPS)
    return (y * g.astype(jnp.float32)).astype(x.dtype)

def layernorm(x, g, b):
    xf = x.astype(jnp.float32)
    mu = jnp.mean(xf, axis=-1, keepdims=True)
    xc = xf - mu
    y = xc * lax.rsqrt(jnp.mean(xc * xc, axis=-1, keepdims=True) + EPS)
    return (y * g.astype(jnp.float32) + b.astype(jnp.float32)).astype(x.dtype)

def sgu_mixer(h, w_in, ln_g, ln_b, w_s, b_s, w_out):
    B_, T, _ = h.shape
    z = jax.nn.gelu(h @ w_in, approximate=False)
    u, v = jnp.split(z, 2, axis=-1)
    v = layernorm(v, ln_g, ln_b)
    n = T // SG_BLOCK
    v = v.reshape(B_, n, SG_BLOCK, SG_GROUPS, SG_GC)
    chunk_id = jnp.arange(SG_BLOCK) // CHUNK
    mask = chunk_id[:, None] >= chunk_id[None, :]
    ws = jnp.where(mask[None], w_s, jnp.zeros((), w_s.dtype))
    s = jnp.einsum('gts,bnsgc->bntgc', ws, v) + b_s.T[None, None, :, :, None]
    y = u * s.reshape(B_, T, SG_WIDTH)
    return y @ w_out

def gla_mixer(h, w_in, w_g2, b_g, gn_g, w_out):
    B_, T, _ = h.shape
    proj = h @ w_in
    q, k, v, r, gz = jnp.split(
        proj, [GLA_KD, 2 * GLA_KD, 2 * GLA_KD + GLA_VD, 2 * GLA_KD + 2 * GLA_VD], axis=-1)
    log_a = jax.nn.log_sigmoid((gz @ w_g2 + b_g).astype(jnp.float32)) / GLA_TAU
    n = T // CHUNK

    def to_chunks(z, d):
        return z.astype(jnp.float32).reshape(B_, n, CHUNK, GLA_HEADS, d).transpose(1, 0, 3, 2, 4)

    qc = to_chunks(q, GLA_DK) * (GLA_DK ** -0.5)
    kc = to_chunks(k, GLA_DK)
    vc = to_chunks(v, GLA_DV)
    Gc = jnp.cumsum(to_chunks(log_a, GLA_DK), axis=3)
    causal = jnp.tril(jnp.ones((CHUNK, CHUNK), dtype=bool))

    def step(S, inp):
        qi, ki, vi, Gi = inp
        diff = Gi[:, :, :, None, :] - Gi[:, :, None, :, :]
        decay = jnp.exp(jnp.where(causal[None, None, :, :, None], diff, -jnp.inf))
        A = jnp.sum(qi[:, :, :, None, :] * ki[:, :, None, :, :] * decay, axis=-1)
        o = jnp.einsum('bhij,bhjv->bhiv', A, vi) + jnp.einsum('bhik,bhkv->bhiv', qi * jnp.exp(Gi), S)
        G_last = Gi[:, :, -1:, :]
        S = jnp.exp(G_last[:, :, 0, :])[..., None] * S + jnp.einsum(
            'bhjk,bhjv->bhkv', ki * jnp.exp(G_last - Gi), vi)
        return S, o

    S0 = jnp.zeros((B_, GLA_HEADS, GLA_DK, GLA_DV), jnp.float32)
    _, o = lax.scan(step, S0, (qc, kc, vc, Gc))
    o = o.transpose(1, 0, 3, 2, 4).reshape(B_, T, GLA_HEADS, GLA_DV)
    o = o * lax.rsqrt(jnp.mean(o * o, axis=-1, keepdims=True) + EPS) * gn_g.astype(jnp.float32)
    o = o.reshape(B_, T, GLA_VD).astype(h.dtype)
    return (jax.nn.silu(r) * o) @ w_out

def swiglu(h, w_gate, w_up, w_down):
    return (jax.nn.silu(h @ w_gate) * (h @ w_up)) @ w_down

def setup_inputs(seed: int = 0) -> dict:
    key = jax.random.key(seed)
    ks = jax.random.split(key, 24)
    na = (DEPTH + 1) // 2
    nb = DEPTH // 2
    f32 = jnp.float32

    def w(k, shape, fan_in):
        return jax.random.normal(k, shape, f32) * (fan_in ** -0.5)

    def gain(k, shape):
        return 1.0 + 0.05 * jax.random.normal(k, shape, f32)

    return {
        "x": jax.random.normal(ks[0], (BATCH, SEQ, D_MODEL), f32),
        "mix_norm": gain(ks[1], (DEPTH, D_MODEL)),
        "a_w_in": w(ks[2], (na, D_MODEL, SG_FFN), D_MODEL),
        "a_ln_g": gain(ks[3], (na, SG_WIDTH)),
        "a_ln_b": 0.02 * jax.random.normal(ks[4], (na, SG_WIDTH), f32),
        "a_w_s": w(ks[5], (na, SG_GROUPS, SG_BLOCK, SG_BLOCK), SG_BLOCK),
        "a_b_s": gain(ks[6], (na, SG_GROUPS, SG_BLOCK)),
        "a_w_out": w(ks[7], (na, SG_WIDTH, D_MODEL), SG_WIDTH),
        "b_w_in": w(ks[8], (nb, D_MODEL, GLA_IN), D_MODEL),
        "b_w_g2": w(ks[9], (nb, GLA_RANK, GLA_KD), GLA_RANK),
        "b_b_g": 0.01 * jax.random.normal(ks[10], (nb, GLA_KD), f32),
        "b_gn_g": gain(ks[11], (nb, GLA_HEADS, GLA_DV)),
        "b_w_out": w(ks[12], (nb, GLA_VD, D_MODEL), GLA_VD),
        "ffn_norm": gain(ks[13], (DEPTH, D_MODEL)),
        "ffn_w_gate": w(ks[14], (DEPTH, D_MODEL, FFN_HIDDEN), D_MODEL),
        "ffn_w_up": w(ks[15], (DEPTH, D_MODEL, FFN_HIDDEN), D_MODEL),
        "ffn_w_down": w(ks[16], (DEPTH, FFN_HIDDEN, D_MODEL), FFN_HIDDEN),
        "final_norm": gain(ks[17], (D_MODEL,)),
    }

def reference(x, mix_norm, a_w_in, a_ln_g, a_ln_b, a_w_s, a_b_s, a_w_out,
              b_w_in, b_w_g2, b_b_g, b_gn_g, b_w_out,
              ffn_norm, ffn_w_gate, ffn_w_up, ffn_w_down, final_norm):
    for i in range(DEPTH):
        h = rmsnorm(x, mix_norm[i])
        j = i // N_MIXERS
        if i % N_MIXERS == 0:
            x = x + sgu_mixer(h, a_w_in[j], a_ln_g[j], a_ln_b[j], a_w_s[j], a_b_s[j], a_w_out[j])
        else:
            x = x + gla_mixer(h, b_w_in[j], b_w_g2[j], b_b_g[j], b_gn_g[j], b_w_out[j])
        h = rmsnorm(x, ffn_norm[i])
        x = x + swiglu(h, ffn_w_gate[i], ffn_w_up[i], ffn_w_down[i])
    return rmsnorm(x, final_norm)


_drawn_inputs = setup_inputs


def setup_inputs(seed=0):
    import zlib

    import numpy as np

    out = dict(_drawn_inputs(seed))
    spreads = {}
    factors = {'a_ln_b': 4.928, 'b_b_g': 8.0, 'b_gn_g': 2.802}
    for name, (base, spread) in spreads.items():
        noise = np.random.default_rng([zlib.crc32(name.encode()), seed]).standard_normal(out[name].shape)
        drawn = base * np.exp(spread * noise) if base else spread * noise
        out[name] = __import__('jax').numpy.asarray(drawn.astype(out[name].dtype))
    for name, factor in factors.items():
        out[name] = (out[name] * factor).astype(out[name].dtype)
    return out
```

```python
from contextlib import ExitStack, contextmanager

import concourse.bass as bass
from concourse import mybir

ALU = mybir.AluOpType
ACT = mybir.ActivationFunctionType
F32 = mybir.dt.float32
F32R = mybir.dt.float32r
U8 = mybir.dt.uint8

P = 128
T = 512
NW = T // P
D = 1024
ND = D // P
CH = 64
SGW = 3 * D
NG = 8
NC_SG = SGW // P
CT_G = NC_SG // NG
NH = 4
DV = D // NH
DK = D // 2 // NH
RANK = 16
TAU = 16.0
HID = 2816
EPS = 1e-6

UK = 2
UC = 512
RING = 4
LEAD = 7
GROUP = 8
LAST = HID // P - 2 * GROUP
NU = ND // UK

LEVELS = [64, 32, 16, 8, 4, 2, 1]
DIAG = len(LEVELS)
MIX0, FFN0, MIX1, FFN1, FINAL = range(5)
GAIN, LN_G, LN_B, GATE_B, GN_G, N_VEC = 0, 40, 64, 88, 92, 100

UNITS = (6 * NU
         + NC_SG // GROUP * (2 * NU + 2 * GROUP // UK)
         + 2 * (11 * NU + 2 * (HID // P) // UK)
         + 7 * NU + 2 * NU)

SETS = []
for _s in range(6):
    SETS.append((f"v{_s}", NU))
for _g in range(3):
    SETS += [(f"u{_g}0", NU), (f"s{_g}0", 0), (f"u{_g}1", NU), (f"s{_g}1", 0),
             (f"so{_g}0", NU), (f"so{_g}1", NU)]


def _swiglu_sets(f):
    for s in range(11):
        SETS.append((f"{f}g{s}", NU))
        if s in (3, 7):
            SETS.extend([(f"{f}o{s}0", NU), (f"{f}o{s}1", NU)])
    SETS.extend([(f"{f}oz0", LAST // UK), (f"{f}oz1", LAST // UK)])


_swiglu_sets("f")
SETS += [("gz", NU), ("q", NU), ("z", 0), ("k", NU), ("gv0", NU), ("L0", 0), ("L1", 0), ("gv1", NU),
         ("L2", 0), ("L3", 0), ("r0", NU), ("KT", 0), ("Ld", 0), ("L4", 0), ("KV0", 0), ("KV1", 0),
         ("L5", 0), ("L6", 0), ("o0", 0), ("o1", 0), ("osum", 0), ("r1", NU), ("go0", NU), ("go1", NU)]
_swiglu_sets("F")
SETS.append(("end", 0))
ROWSUMS = 1
INDEX = {name: n + ROWSUMS for n, (name, _) in enumerate(SETS)}


def bank(name):
    return 4 * (INDEX[name] % 2)


def units_through(name):
    return sum(n for _, n in SETS[:INDEX[name] - ROWSUMS + 1])


def turned_through(name):
    return ROWSUMS + sum(n == 0 for _, n in SETS[:INDEX[name] - ROWSUMS + 1])


class Count:

    def __init__(self, n=0):
        self.n, self.i, self.per = n, None, 0

    def add(self, k=1):
        self.n += k
        return self.value()

    def value(self, more=0):
        return self.n + more if self.i is None else self.i * self.per + (self.n + more)


@contextmanager
def turns(eng, times, *counts):
    before = [c.n for c, _ in counts]
    with eng.Fori(0, times) as i:
        for c, per in counts:
            c.i, c.per = i, per
        yield i
    for (c, per), n in zip(counts, before):
        assert c.n == n + per, "a count grew by another amount than stated"
        c.i, c.n = None, n + per * times


def build_trunk(nc, x_T, weights, spatial_T, spatial_bias, vectors, w_g2, level_masks, identity, out_T):
    with ExitStack() as ctx:
        top = [(nc.sbuf_base + 31) // 32 * 32]

        def place(name, shape, dt=F32, over=None):
            at = top[0] if over is None else over
            words = 1
            for s in shape[1:]:
                words *= s
            if over is None:
                top[0] = at + (words * (1 if dt == U8 else 4) + 31) // 32 * 32
            t = nc.alloc_sbuf_tensor_at(name, shape, dt, offset=at)
            return t, at

        xT, _ = place("xT", [P, ND, T])
        h_hi, _ = place("h_hi", [P, ND, T], F32R)
        h_lo, _ = place("h_lo", [P, ND, T], F32R)
        y_hi, at_yhi = place("y_hi", [P, GROUP, T], F32R)
        y_lo, at_ylo = place("y_lo", [P, GROUP, T], F32R)
        raw, _ = place("raw", [P, RING, UK * UC])
        w_hi, _ = place("w_hi", [P, RING, UK * UC], F32R)
        w_lo, _ = place("w_lo", [P, RING, UK * UC], F32R)
        arena, _ = place("arena", [P, 17 * 1024])
        sumsq, _ = place("sumsq", [P, T])
        square, _ = place("square", [P, T])
        rstd_row, _ = place("rstd_row", [P, T])
        ident, _ = place("ident", [P, P])
        ones, _ = place("ones", [P, P])
        masks, _ = place("masks", [P, DIAG + 1, P], U8)
        vec, _ = place("vec", [P, N_VEC])
        rstd_col, _ = place("rstd_col", [P, NW])
        eps, _ = place("eps", [P, 1])
        stats, _ = place("stats", [P, NW, 6, 6])
        moments, _ = place("moments", [P, NW, 2])
        ln_rstd, _ = place("ln_rstd", [P, NW])
        glast, _ = place("glast", [P, NH, NW])
        state, _ = place("state", [P, NH, NW - 1, DV], over=at_yhi)
        v_gla, _ = place("v_gla", [P, NW, D], over=at_ylo)
        ps = ctx.enter_context(nc.psum_tensor("ps", [P, 8, T], F32))

        def region(at, a, b):
            return arena[:, at * 1024:at * 1024 + a * b].rearrange("p (a b) -> p a b", a=a)

        v_sg = region(0, NW, SGW)
        masks_in = region(0, DIAG + 1, P)
        ws_T = region(12, NG, P)
        ws_rows = region(13, NG, P)
        bias_s = region(14, NG, P)
        pair = region(15, 4, T)
        s_bias = square[:].rearrange("p (j t) -> p j t", j=4)
        q_T = region(0, NH, T)
        k_T = region(2, NH, T)
        G_T = region(4, NH, T)
        QK = [region(6, NH, T), region(8, NH, T)]
        A_T = region(10, NH, T)
        gate_T = [region(12, NH, T), region(2, NH, T)]
        k_nat = region(14, NH, T)
        rstd_o = region(14, NH, T)
        g2_sb = arena[0:RANK, 16 * 1024:16 * 1024 + NH * DK]
        gz_T = arena[0:RANK, 16 * 1024 + T:17 * 1024]
        o_T = [QK[1], QK[0]]
        o_sq = [q_T, G_T]
        result = region(0, ND, T)

        def sem(name):
            return ctx.enter_context(nc.semaphore(name))

        landed = [sem(f"weights_landed_{i}") for i in range(RING)]
        hi_ready = sem("hi_ready")
        lo_ready = sem("lo_ready")
        units_used = sem("units_used")
        turned = sem("turned")
        banks_free = sem("banks_free")
        x_landed = [sem(f"x_landed_{i}") for i in range(2)]
        spatial_landed = sem("spatial_landed")
        vec_landed = sem("vec_landed")
        late_landed = sem("late_landed")
        g2_landed = sem("g2_landed")
        consts_ready = sem("consts_ready")
        x_ready = sem("x_ready")
        hhi_ready = sem("hhi_ready")
        hlo_ready = sem("hlo_ready")
        sq_ready = sem("sq_ready")
        sum_ready = sem("sum_ready")
        norm_sums = sem("norm_sums")
        root_ready = sem("root_ready")
        rstd_ready = sem("rstd_ready")
        dve_own = sem("dve_own")
        act_own = sem("act_own")
        pre_ready = sem("pre_ready")
        fn_ready = sem("fn_ready")
        y_ready = sem("y_ready")
        yhi_ready = sem("yhi_ready")
        ylo_ready = sem("ylo_ready")
        v_ready = sem("v_ready")
        stats_ready = sem("stats_ready")
        var_ready = sem("var_ready")
        std_ready = sem("std_ready")
        vhat_ready = sem("vhat_ready")
        softplus_ready = sem("softplus_ready")
        diff_ready = sem("diff_ready")
        exp_ready = sem("exp_ready")
        qk_ready = sem("qk_ready")
        glast_ready = sem("glast_ready")
        o_ready = sem("o_ready")
        osq_ready = sem("osq_ready")
        opair_ready = sem("opair_ready")
        oroot_ready = sem("oroot_ready")
        out_ready = sem("out_ready")
        out_stored = sem("out_stored")

        block = ctx.enter_context(nc.Block())

        @block.sync
        def _(sp):
            for half in range(2):
                sp.dma_start(xT[:, 4 * half:4 * half + 4, :], x_T[:, 4 * half:4 * half + 4, :]).then_inc(
                    x_landed[half], 16)
                sp.dma_start(raw[:, half, :], weights[half]).then_inc(landed[half], 16)
            for slot in range(2, RING):
                sp.dma_start(raw[:, slot, :], weights[slot]).then_inc(landed[slot], 16)
            issued = Count(RING)
            with turns(sp, UNITS // RING - 1, (issued, RING)) as i:
                for slot in range(RING):
                    sp.wait_ge(lo_ready, issued.value(1 - RING))
                    sp.dma_start(raw[:, slot, :], weights[bass.ds(i * RING + (RING + slot), 1), :, :].rearrange(
                        "u p c -> p (u c)")).then_inc(landed[slot], 16)
                    issued.add()
            for tile in range(ND):
                sp.wait_ge(out_ready, tile + 1)
                sp.dma_start(out_T[tile * P:(tile + 1) * P, :], result[:, tile, :]).then_inc(out_stored, 16)
            sp.wait_ge(out_stored, 16 * ND)

        @block.gpsimd
        def _(pool):
            pool.dma_start(ws_T[0:CH], spatial_T[0:CH]).then_inc(spatial_landed, 16)
            pool.dma_start(ws_T[CH:P, :, CH:P], spatial_T[CH:P, :, CH:P]).then_inc(spatial_landed, 16)
            pool.dma_start(bias_s, spatial_bias.partition_broadcast(P)).then_inc(late_landed, 16)
            pool.dma_start(masks_in, level_masks).then_inc(late_landed, 16)
            pool.dma_start(ident[:], identity).then_inc(late_landed, 16)
            nc.gpsimd.memset(ones[:], 1.0).then_inc(consts_ready, 1)
            pool.wait_ge(consts_ready, 1)
            nc.gpsimd.memset(eps[:], EPS).then_inc(consts_ready, 1)
            pool.wait_ge(consts_ready, 2)
            nc.gpsimd.memset(ws_T[CH:P, :, 0:CH], 0.0).then_inc(consts_ready, 1)
            pool.wait_ge(consts_ready, 3)
            pool.wait_ge(late_landed, 48)
            nc.gpsimd.tensor_copy(masks[:], masks_in).then_inc(consts_ready, 1)
            for n in range(5 * ND):
                pool.wait_ge(sq_ready, n + 1)
                if n % ND == 0:
                    nc.gpsimd.tensor_copy(sumsq[:], square[:]).then_inc(sum_ready, 1)
                else:
                    pool.wait_ge(sum_ready, n)
                    nc.gpsimd.tensor_tensor(sumsq[:], sumsq[:], square[:], ALU.add).then_inc(sum_ready, 1)

        @block.tensor
        def _(pe):
            used = Count()
            sets = Count()
            y_seen = Count()
            norms = Count()
            h_before = Count()

            def open_set():
                b = 4 * (sets.n % 2)
                if sets.i is not None or sets.n >= 2:
                    pe.wait_ge(banks_free, sets.value(-1))
                sets.add()
                return b

            def three_passes(acc, w_h, w_l, o_h, o_l, weights_stationary, start, stop):
                if weights_stationary:
                    nc.tensor.matmul(acc, w_h, o_l, start=start, stop=False)
                    nc.tensor.matmul(acc, w_h, o_h, start=False, stop=False)
                    return nc.tensor.matmul(acc, w_l, o_h, start=False, stop=stop)
                nc.tensor.matmul(acc, o_h, w_l, start=start, stop=False)
                nc.tensor.matmul(acc, o_h, w_h, start=False, stop=False)
                return nc.tensor.matmul(acc, o_l, w_h, start=False, stop=stop)

            def norm_matmuls(b):
                pe.wait_ge(sum_ready, norms.add() * ND)
                nc.tensor.matmul(ps[:, b + 3, :], ones[:], sumsq[:], start=True, stop=True)
                for w in range(NW):
                    m = nc.tensor.matmul(ps[:, b + 2, w:w + 1], sumsq[:, w * P:(w + 1) * P], ones[:, 0:1],
                                         start=True, stop=True)
                m.then_inc(norm_sums, 1)

            def product_set(hi, lo, nk, natural=False, tiles=4, wait_h=False, wait_y=False,
                            norm_inside=False, norm_before=False, inside=None):
                b = open_set()
                for k in range(0, nk, UK):
                    pe.wait_ge(lo_ready, used.value(1))
                    if wait_h:
                        pe.wait_ge(hlo_ready, h_before.n + k + UK)
                    if wait_y:
                        pe.wait_ge(ylo_ready, y_seen.value(k + UK))
                    if inside is not None and k == 2 * UK:
                        inside()
                    slot = used.n % RING
                    for t in range(tiles):
                        if norm_before and k == 0 and t == 2:
                            pe.wait_ge(root_ready, norms.n)
                        if norm_inside and k == nk - UK and t == 2:
                            pe.wait_ge(banks_free, sets.n - 1)
                            norm_matmuls(4 - b)
                        for j in range(UK):
                            start, stop = k + j == 0, k + j == nk - 1
                            if natural:
                                c, o = slice(j * UC, (j + 1) * UC), slice(t * P, (t + 1) * P)
                            else:
                                c, o = slice(j * UC + t * P, j * UC + (t + 1) * P), slice(0, T)
                            m = three_passes(ps[:, b + t, :], w_hi[:, slot, c], w_lo[:, slot, c],
                                             hi[:, k + j, o], lo[:, k + j, o], not natural, start, stop)
                    m.then_inc(units_used, 1)
                    used.add()

            def in_set(**kw):
                product_set(h_hi, h_lo, ND, **kw)

            def out_sets(nk):
                for _ in range(2):
                    product_set(y_hi, y_lo, nk, wait_y=True)
                y_seen.add(nk)

            b = open_set()
            pe.wait_ge(spatial_landed, 32)
            pe.wait_ge(consts_ready, 3)
            for n in range(2):
                m = nc.tensor.matmul(ps[:, b + n, :], ones[:], ws_T[:, 4 * n:4 * n + 4, :], start=True, stop=True)
            m.then_inc(turned, 1)

            in_set(natural=True, wait_h=True, norm_inside=True)
            in_set(natural=True, norm_before=True)
            with turns(pe, 2, (used, 2 * NU), (sets, 2)):
                in_set(natural=True)
                in_set(natural=True)
            for g in range(NC_SG // GROUP):
                for s in range(2):
                    in_set()
                    b = open_set()
                    pe.wait_ge(vhat_ready, NW)
                    for j in range(4):
                        c = g * GROUP + 4 * s + j
                        for w in range(NW):
                            m = nc.tensor.matmul(ps[:, b + j, w * P:(w + 1) * P], v_sg[:, w, c * P:(c + 1) * P],
                                                 ws_T[:, c // CT_G, :], start=True, stop=True)
                    m.then_inc(turned, 1)
                out_sets(GROUP)

            def swiglu():
                h_before.add(ND)
                in_set(wait_h=True, norm_inside=True)
                in_set(norm_before=True)
                in_set()
                in_set()
                out_sets(GROUP)
                for _ in range(4):
                    in_set()
                out_sets(GROUP)
                for _ in range(3):
                    in_set()
                out_sets(LAST)

            swiglu()

            h_before.add(ND)
            in_set(tiles=1, wait_h=True)
            pe.wait_ge(banks_free, sets.n - 1)
            norm_matmuls(4 * (sets.n % 2))
            in_set(norm_before=True)
            b = open_set()
            pe.wait_ge(banks_free, INDEX["gz"] + 1)
            pe.wait_ge(g2_landed, 16)
            for h in range(NH):
                m = nc.tensor.matmul(ps[:, b + h, :], g2_sb[:, h * P:(h + 1) * P], gz_T, start=True, stop=True)
            m.then_inc(turned, 1)
            in_set()

            def pairs(lhs, rhs):
                b = 4 * ((sets.n - 1) % 2)
                for h in range(NH):
                    for w in range(NW):
                        c = slice(w * P, (w + 1) * P)
                        m = nc.tensor.matmul(ps[:, b + h, c], lhs[:, h, c], rhs[:, h, c], start=True, stop=True)
                m.then_inc(turned, 1)

            def level(item):
                open_set()
                pe.wait_ge(qk_ready, item + 1)
                pairs(QK[item % 2], QK[item % 2])

            in_set(natural=True)
            level(0)
            level(1)
            in_set(natural=True)
            level(2)
            level(3)
            in_set()
            b = open_set()
            pe.wait_ge(qk_ready, 5)
            pe.wait_ge(late_landed, 48)
            for h in range(NH):
                for w in range(NW - 1):
                    c = slice(w * P, (w + 1) * P)
                    m = nc.tensor.transpose(ps[:, b + h, c], QK[0][:, h, c], ident[:])
            m.then_inc(turned, 1)
            open_set()
            pe.wait_ge(banks_free, INDEX["k"] + 1)
            pairs(k_T, q_T)
            level(5)
            for part, windows in enumerate(((0, 1), (2,))):
                b = open_set()
                pe.wait_ge(banks_free, INDEX["KT"] + 1)
                pe.wait_ge(v_ready, 8 * NW)
                for h in range(NH):
                    for n, w in enumerate(windows):
                        m = nc.tensor.matmul(ps[:, b + h, n * DV:(n + 1) * DV], k_nat[:, h, w * P:(w + 1) * P],
                                             v_gla[:, w, h * DV:(h + 1) * DV], start=True, stop=True)
                m.then_inc(turned, 1)
            level(6)
            level(7)
            for part in range(2):
                b = open_set()
                pe.wait_ge(banks_free, INDEX["L6"] + 1)
                pe.wait_ge(banks_free, INDEX["KV1"] + 1)
                pe.wait_ge(qk_ready, 9)
                for j in range(4):
                    h, v0 = 2 * part + j // 2, j % 2 * P
                    for w in range(NW):
                        c = slice(w * P, (w + 1) * P)
                        m = nc.tensor.matmul(ps[:, b + j, c], v_gla[:, w, h * DV + v0:h * DV + v0 + P], A_T[:, h, c],
                                             start=True, stop=w == 0)
                        if w:
                            m = nc.tensor.matmul(ps[:, b + j, c], state[:, h, w - 1, v0:v0 + P], QK[0][:, h, c],
                                                 start=False, stop=True)
                m.then_inc(turned, 1)
            o_bank = open_set()

            def head_sums():
                pe.wait_ge(opair_ready, NH)
                for h in range(NH):
                    m = nc.tensor.matmul(ps[:, o_bank + h, :], ones[:], o_sq[h // 2][:, 2 * (h % 2), :],
                                         start=True, stop=True)
                m.then_inc(turned, 1)

            in_set(inside=head_sums)
            out_sets(ND)

            swiglu()
            b = open_set()
            norm_matmuls(b)

        @block.scalar
        def _(act):
            unit = Count()
            x_seen, pre, y_seen, norms, squares, diffs = (Count() for _ in range(6))

            def split():
                if unit.i is None and unit.n >= UNITS:
                    return
                slot, rounds = unit.n % RING, 16 * (unit.n // RING + 1)
                act.wait_ge(landed[slot], rounds if unit.i is None else unit.i * (16 * unit.per // RING) + rounds)
                if unit.i is not None or unit.n >= RING:
                    act.wait_ge(units_used, unit.value(1 - RING))
                nc.scalar.copy(w_hi[:, slot, :], raw[:, slot, :]).then_inc(hi_ready, 1)
                unit.add()

            def drain(n, piece=None):
                for j in range(4):
                    if j < n - n % 2:
                        split()
                    if piece is not None:
                        piece(j)
                if n % 2:
                    split()

            def drain_before_turned(piece):
                split()
                for j in range(4):
                    piece(j)

            def splits_put_off():
                for _ in range(NU - 1):
                    split()

            def finish_norm(b):
                act.wait_ge(norm_sums, norms.add())
                nc.scalar.activation(rstd_col[:], ps[:, b + 2, 0:NW], ACT.Sqrt, bias=eps[:, 0:1], scale=1.0 / D)
                nc.scalar.activation(rstd_row[:], ps[:, b + 3, :], ACT.Sqrt, bias=eps[:, 0:1],
                                     scale=1.0 / D).then_inc(root_ready, 1)

            def square_tile(tile):
                if squares.n:
                    act.wait_ge(sum_ready, squares.n)
                nc.scalar.activation(square[:], xT[:, tile, :], ACT.Square).then_inc(sq_ready, 1)
                squares.add()

            def operand_tile(tile, gain):
                nc.scalar.activation(h_hi[:, tile, :], xT[:, tile, :], ACT.Copy,
                                     scale=vec[:, GAIN + gain * ND + tile:GAIN + gain * ND + tile + 1]).then_inc(
                                         hhi_ready, 1)
                square_tile(tile)

            def drain_out(n, gain):
                for half in range(2):
                    def piece(j):
                        if gain is None:
                            x_seen.add()
                            return
                        act.wait_ge(x_ready, x_seen.add())
                        if gain == FINAL:
                            square_tile(4 * half + j)
                        else:
                            operand_tile(4 * half + j, gain)
                    drain(n, piece)

            def upper_y(tile, source):
                act.wait_ge(y_ready, y_seen.add())
                nc.scalar.copy(y_hi[:, tile, :], source).then_inc(yhi_ready, 1)

            def function(tile, f):
                act.wait_ge(pre_ready, pre.add())
                nc.scalar.activation(tile, tile, f).then_inc(fn_ready, 1)

            act.dma_start(vec[:], vectors).then_inc(vec_landed, 16)
            act.wait_ge(vec_landed, 16)
            act.wait_ge(consts_ready, 3)
            for tile in range(ND):
                if tile % 4 == 0:
                    act.wait_ge(x_landed[tile // 4], 16)
                operand_tile(tile, MIX0)
                if tile < RING - 1:
                    split()
            for _ in range(LEAD - RING + 1):
                split()

            finish_norm(bank("v1"))
            act.wait_ge(rstd_ready, norms.n)
            act.wait_ge(consts_ready, 4)
            with turns(act, 3, (unit, 2 * NU)) as i:
                for s in range(2):
                    b = bank(f"v{s}")

                    def piece(w):
                        nc.scalar.activation(v_sg[:, w, bass.ds(i * (2 * UC) + s * UC, UC)], ps[:, b + w, :],
                                             ACT.Gelu, scale=rstd_col[:, w:w + 1]).then_inc(v_ready, 1)
                    drain(NU, piece)
            act.wait_ge(var_ready, 1)
            nc.scalar.activation(ln_rstd[:], moments[:, :, 1], ACT.Sqrt, bias=eps[:, 0:1]).then_inc(std_ready, 1)

            for g in range(NC_SG // GROUP):
                for s in range(2):
                    drain_before_turned(lambda j: function(pair[:, j, :], ACT.Gelu))
                    for j in range(4):
                        upper_y(4 * s + j, pair[:, j, :])
                    splits_put_off()
                drain_out(GROUP // UK, FFN0 if g == 2 else None)

            def gate_up(tile0):
                for j in range(2):
                    split()
                    function(pair[:, j, :], ACT.Silu)
                split()
                for j in range(2):
                    upper_y(tile0 + j, pair[:, j, :])
                split()

            def swiglu(f, gain):
                finish_norm(bank(f + "g1"))
                gate_up(0)
                with turns(act, 2, (unit, 24), (pre, 8), (y_seen, 8), (x_seen, ND)):
                    for s in range(1, 4):
                        gate_up(2 * s)
                    drain_out(GROUP // UK, None)
                    gate_up(0)
                for s in range(1, 3):
                    gate_up(2 * s)
                drain_out(LAST // UK, gain)

            swiglu("f", MIX1)

            act.wait_ge(ylo_ready, y_seen.n)
            act.dma_start(g2_sb, w_g2).then_inc(g2_landed, 16)
            finish_norm(bank("q"))
            drain(NU)
            split()
            act.wait_ge(banks_free, INDEX["z"] + 1)
            nc.scalar.activation(QK[0], G_T, ACT.Abs).then_inc(act_own, 1)
            act.wait_ge(act_own, 1)
            nc.scalar.activation(QK[0], QK[0], ACT.Exp, scale=-1.0).then_inc(act_own, 1)
            act.wait_ge(act_own, 2)
            nc.scalar.activation(QK[0], QK[0], ACT.Ln, bias=ones[:, 0:1]).then_inc(softplus_ready, 1)
            splits_put_off()

            def exponential():
                buf = QK[diffs.n % 2]
                act.wait_ge(diff_ready, diffs.add())
                nc.scalar.activation(buf, buf, ACT.Exp, scale=1.0 / TAU).then_inc(exp_ready, 1)

            exponential()
            exponential()
            nc.scalar.activation(glast[:], G_T[:, :, P - 1::P], ACT.Exp, scale=1.0 / TAU).then_inc(glast_ready, 1)
            drain(NU)

            def v_pieces(half):
                name = f"gv{half}"

                def piece(w):
                    if w == 0:
                        act.wait_ge(units_used, units_through(name))
                    nc.scalar.activation(v_gla[:, w, half * UC:(half + 1) * UC], ps[:, bank(name) + w, :], ACT.Copy,
                                         scale=rstd_col[:, w:w + 1]).then_inc(v_ready, 1)
                drain_before_turned(piece)

            v_pieces(0)
            exponential()
            exponential()
            splits_put_off()
            v_pieces(1)
            exponential()
            exponential()
            splits_put_off()
            drain_before_turned(lambda j: function(gate_T[0][:, j, :], ACT.Silu))
            for _ in range(3):
                exponential()
            for t in range(ND):
                act.wait_ge(o_ready, t + 1)
                nc.scalar.activation(o_sq[t // 4][:, t % 4, :], o_T[t // 4][:, t % 4, :], ACT.Square).then_inc(
                    osq_ready, 1)
            act.wait_ge(turned, turned_through("osum"))
            for h in range(NH):
                nc.scalar.activation(rstd_o[:, h, :], ps[:, bank("osum") + h, :], ACT.Sqrt, bias=eps[:, 0:1],
                                     scale=1.0 / DV).then_inc(oroot_ready, 1)
            for t in range(4):
                upper_y(t, o_T[0][:, t, :])
            splits_put_off()
            drain_before_turned(lambda j: function(gate_T[1][:, j, :], ACT.Silu))
            for t in range(4):
                upper_y(4 + t, o_T[1][:, t, :])
            splits_put_off()
            drain_out(NU, FFN1)

            swiglu("F", FINAL)
            finish_norm(bank("end"))

        @block.vector
        def _(dve):
            unit = Count()
            drained = Count()
            sets = Count()
            x_done, h_done, pre, y_done, norms, v_seen, own, products = (Count() for _ in range(8))

            def split():
                if unit.i is None and unit.n >= UNITS:
                    return
                slot = unit.n % RING
                dve.wait_ge(hi_ready, unit.value(1))
                nc.vector.tensor_tensor(w_lo[:, slot, :], raw[:, slot, :], w_hi[:, slot, :].bitcast(F32),
                                        ALU.subtract).then_inc(lo_ready, 1)
                unit.add()

            def product_banks(n):
                b = 4 * (sets.n % 2)
                dve.wait_ge(units_used, drained.add(n))
                sets.add()
                return b

            def turned_banks(name):
                b = 4 * (sets.n % 2)
                assert sets.i is not None or sets.n == INDEX[name]
                dve.wait_ge(turned, turned_through(name))
                sets.add()
                return b

            def after_own(ins):
                ins.then_inc(dve_own, 1)
                dve.wait_ge(dve_own, own.add())

            def finish_norm():
                dve.wait_ge(root_ready, norms.add())
                nc.vector.reciprocal(rstd_col[:], rstd_col[:])
                nc.vector.reciprocal(rstd_row[:], rstd_row[:]).then_inc(rstd_ready, 1)
                dve.wait_ge(rstd_ready, norms.n)

            def lower_h(tile, gain):
                dve.wait_ge(hhi_ready, h_done.add())
                nc.vector.scalar_tensor_tensor(out=h_lo[:, tile, :], in0=xT[:, tile, :],
                                               scalar=vec[:, GAIN + gain * ND + tile:GAIN + gain * ND + tile + 1],
                                               in1=h_hi[:, tile, :].bitcast(F32), op0=ALU.mult,
                                               op1=ALU.subtract).then_inc(hlo_ready, 1)

            def drain_out(n, gain):
                for half in range(2):
                    b = None
                    for j in range(4):
                        if j < n - n % 2:
                            split()
                        if b is None:
                            b = product_banks(n)
                        tile = 4 * half + j
                        nc.vector.tensor_tensor(xT[:, tile, :], ps[:, b + j, :], xT[:, tile, :], ALU.add).then_inc(
                            x_ready, 1)
                        x_done.add()
                        if gain not in (None, FINAL) and j > 0:
                            lower_h(tile - 1, gain)
                    dve.wait_ge(x_ready, x_done.value())
                    dve.sem_inc(banks_free, 1)
                    if gain not in (None, FINAL):
                        lower_h(4 * half + 3, gain)
                    if n % 2:
                        split()

            def lower_y(tile, source):
                dve.wait_ge(yhi_ready, y_done.add())
                nc.vector.tensor_tensor(y_lo[:, tile, :], source, y_hi[:, tile, :].bitcast(F32),
                                        ALU.subtract).then_inc(ylo_ready, 1)

            def splits_put_off():
                for _ in range(NU - 1):
                    split()

            dve.wait_ge(vec_landed, 16)
            dve.wait_ge(x_landed[0], 16)
            for tile in range(ND):
                if tile == 4:
                    dve.wait_ge(x_landed[1], 16)
                lower_h(tile, MIX0)
                if tile < RING - 1:
                    split()
            b = 4 * (sets.n % 2)
            dve.wait_ge(turned, 1)
            nc.vector.tensor_copy(ws_rows.rearrange("p g t -> p (g t)"),
                                  ps[:, b:b + 2, :].rearrange("p a t -> p (a t)")).then_inc(banks_free, 1)
            sets.add()
            for _ in range(LEAD - RING + 1):
                split()

            finish_norm()
            with turns(dve, 3, (unit, 2 * NU), (drained, 2 * NU), (sets, 2), (v_seen, 2 * NW)) as i:
                for s in range(2):
                    for w in range(NW):
                        dve.wait_ge(v_ready, v_seen.add())
                        split()
                        nc.vector.bn_stats(stats[:, w, bass.ds(i * 2 + s, 1), :].rearrange("p a s -> p (a s)"),
                                           v_sg[:, w, bass.ds(i * (2 * UC) + s * UC, UC)]).then_inc(stats_ready, 1)
                    dve.sem_inc(banks_free, 1)
                    drained.add(NU)
                    sets.add()
            dve.wait_ge(stats_ready, 6 * NW)
            for w in range(NW):
                m = nc.vector.bn_aggr(moments[:, w, :], stats[:, w, :, :].rearrange("p a s -> p (a s)"))
            m.then_inc(var_ready, 1)
            dve.wait_ge(std_ready, 1)
            after_own(nc.vector.reciprocal(ln_rstd[:], ln_rstd[:]))
            for w in range(NW):
                nc.vector.tensor_scalar(v_sg[:, w, :], v_sg[:, w, :], moments[:, w, 0:1], ln_rstd[:, w:w + 1],
                                        ALU.subtract, ALU.mult).then_inc(vhat_ready, 1)

            dve.wait_ge(late_landed, 48)
            for g in range(NC_SG // GROUP):
                for s in range(2):
                    split()
                    b = product_banks(NU)
                    if y_done.n:
                        dve.wait_ge(ylo_ready, y_done.n)
                    for j in range(4):
                        nc.vector.tensor_tensor(pair[:, j, :], ps[:, b + j, :], rstd_row[:], ALU.mult).then_inc(
                            pre_ready, 1)
                        pre.add()
                    for j in range(4):
                        c = g * GROUP + 4 * s + j
                        m = nc.vector.scalar_tensor_tensor(
                            out=s_bias[:, j, :], in0=ws_rows[:, c // CT_G, :], scalar=vec[:, LN_B + c:LN_B + c + 1],
                            in1=bias_s[:, c // CT_G, :], op0=ALU.mult, op1=ALU.add)
                    after_own(m)
                    dve.wait_ge(fn_ready, pre.n)
                    dve.sem_inc(banks_free, 1)
                    b = turned_banks(f"s{g}{s}")
                    for j in range(4):
                        c = g * GROUP + 4 * s + j
                        acc = ps[:, b + j, :].rearrange("p (w t) -> p w t", w=NW)
                        m = nc.vector.scalar_tensor_tensor(
                            out=acc, in0=acc, scalar=vec[:, LN_G + c:LN_G + c + 1],
                            in1=s_bias[:, j:j + 1, :].broadcast_to([P, NW, P]), op0=ALU.mult, op1=ALU.add)
                    after_own(m)
                    for j in range(4):
                        nc.vector.tensor_tensor(pair[:, j, :], ps[:, b + j, :], pair[:, j, :], ALU.mult).then_inc(
                            y_ready, 1)
                    for j in range(4):
                        lower_y(4 * s + j, pair[:, j, :])
                    dve.sem_inc(banks_free, 1)
                    splits_put_off()
                drain_out(GROUP // UK, FFN0 if g == 2 else None)

            def gate_up(tile0):
                def scale(j):
                    nc.vector.tensor_tensor(pair[:, 2 + j, :], ps[:, b + 2 + j, :], rstd_row[:], ALU.mult)
                    nc.vector.tensor_tensor(pair[:, j, :], ps[:, b + j, :], rstd_row[:], ALU.mult).then_inc(
                        pre_ready, 1)
                    pre.add()

                def multiply(j):
                    dve.wait_ge(fn_ready, pre.value(j - 1))
                    nc.vector.tensor_tensor(pair[:, j, :], pair[:, j, :], pair[:, 2 + j, :], ALU.mult).then_inc(
                        y_ready, 1)

                split()
                b = product_banks(NU)
                dve.wait_ge(ylo_ready, y_done.value())
                scale(0)
                split()
                scale(1)
                multiply(0)
                split()
                multiply(1)
                dve.sem_inc(banks_free, 1)
                lower_y(tile0, pair[:, 0, :])
                lower_y(tile0 + 1, pair[:, 1, :])
                split()

            def swiglu(gain):
                finish_norm()
                gate_up(0)
                with turns(dve, 2, (unit, 24), (drained, 24), (sets, 6), (pre, 8), (y_done, 8), (x_done, ND)):
                    for s in range(1, 4):
                        gate_up(2 * s)
                    drain_out(GROUP // UK, None)
                    gate_up(0)
                for s in range(1, 3):
                    gate_up(2 * s)
                drain_out(LAST // UK, gain)

            swiglu(MIX1)

            finish_norm()
            for _ in range(NU):
                split()
            b = product_banks(NU)
            dve.wait_ge(g2_landed, 16)
            nc.vector.tensor_tensor(gz_T, ps[0:RANK, b, :], rstd_row[0:RANK, :], ALU.mult).then_inc(banks_free, 1)
            split()
            b = product_banks(NU)
            for h in range(NH):
                m = nc.vector.scalar_tensor_tensor(out=q_T[:, h, :], in0=ps[:, b + h, :], scalar=float(DK) ** -0.5,
                                                   in1=rstd_row[:], op0=ALU.mult, op1=ALU.mult)
            m.then_inc(banks_free, 1)
            b = turned_banks("z")
            for h in range(NH):
                m = nc.vector.tensor_scalar(G_T[:, h, :], ps[:, b + h, :], vec[:, GATE_B + h:GATE_B + h + 1], None,
                                            ALU.add)
            m.then_inc(banks_free, 1)
            after_own(nc.vector.memset(A_T, 0.0))
            dve.wait_ge(softplus_ready, 1)
            after_own(nc.vector.scalar_tensor_tensor(out=QK[1], in0=G_T, scalar=0.0, in1=QK[0], op0=ALU.min,
                                                     op1=ALU.subtract))
            splits_put_off()
            for h in range(NH):
                for w in range(NW):
                    c = slice(w * P, (w + 1) * P)
                    m = nc.vector.tensor_tensor_scan(G_T[:, h, c], ones[:], QK[1][:, h, c], 0.0, ALU.mult, ALU.add)
            after_own(m)

            def halves(x, m):
                v = x.rearrange("p h (n s) -> p (h n) s", s=2 * m)
                return v[:, :, 0:m], v[:, :, m:2 * m]

            def differences(item):
                buf = QK[item % 2]
                kind = ITEMS[item]
                if kind == "end":
                    g = G_T.rearrange("p h (n s) -> p (h n) s", s=P)
                    nc.vector.tensor_tensor(buf.rearrange("p h (n s) -> p (h n) s", s=P),
                                            g[:, :, P - 1:P].broadcast_to([P, NH * NW, P]), g,
                                            ALU.subtract).then_inc(diff_ready, 1)
                elif kind == "start":
                    nc.vector.tensor_copy(buf, G_T).then_inc(diff_ready, 1)
                else:
                    g_early, g_late = halves(G_T, kind)
                    early, late = halves(buf, kind)
                    middle = g_early[:, :, kind - 1:kind].broadcast_to([P, NH * T // (2 * kind), kind])
                    nc.vector.tensor_tensor(late, g_late, middle, ALU.subtract)
                    nc.vector.tensor_tensor(early, middle, g_early, ALU.subtract).then_inc(diff_ready, 1)

            def decayed(item):
                buf = QK[item % 2]
                kind = ITEMS[item]
                dve.wait_ge(exp_ready, item + 1)
                if kind == "end":
                    nc.vector.tensor_tensor(buf, buf, k_T, ALU.mult).then_inc(qk_ready, 1)
                elif kind == "start":
                    nc.vector.tensor_tensor(buf, buf, q_T, ALU.mult).then_inc(qk_ready, 1)
                else:
                    early, late = halves(buf, kind)
                    nc.vector.tensor_tensor(late, late, halves(q_T, kind)[1], ALU.mult)
                    nc.vector.tensor_tensor(early, early, halves(k_T, kind)[0], ALU.mult).then_inc(qk_ready, 1)

            def take_level(name, mask):
                dve.wait_ge(banks_free, INDEX[name])
                b = turned_banks(name)
                for h in range(NH):
                    m = nc.vector.copy_predicated(
                        A_T[:, h, :].rearrange("p (w t) -> p w t", w=NW),
                        masks[:, mask:mask + 1, :].broadcast_to([P, NW, P]),
                        ps[:, b + h, :].rearrange("p (w t) -> p w t", w=NW))
                m.then_inc(banks_free, 1)

            def gate(part):
                split()
                b = product_banks(NU)
                for j in range(4):
                    nc.vector.tensor_tensor(gate_T[part][:, j, :], ps[:, b + j, :], rstd_row[:], ALU.mult).then_inc(
                        pre_ready, 1)
                    pre.add()

            def pass_v(half):
                split()
                product_banks(NU)
                dve.wait_ge(v_ready, (6 + half + 1) * NW)
                dve.sem_inc(banks_free, 1)

            differences(0)
            differences(1)
            for h in range(NH):
                split()
                if h == 0:
                    b = product_banks(NU)
                m = nc.vector.tensor_tensor(k_T[:, h, :], ps[:, b + h, :], rstd_row[:], ALU.mult)
            m.then_inc(banks_free, 1)
            dve.wait_ge(banks_free, INDEX["k"] + 1)
            decayed(0)
            decayed(1)
            pass_v(0)
            take_level("L0", 0)
            differences(2)
            take_level("L1", 1)
            differences(3)
            decayed(2)
            decayed(3)
            splits_put_off()
            pass_v(1)
            take_level("L2", 2)
            differences(4)
            take_level("L3", 3)
            differences(5)
            decayed(4)
            decayed(5)
            splits_put_off()
            gate(0)
            dve.wait_ge(fn_ready, pre.n)
            dve.sem_inc(banks_free, 1)
            b = turned_banks("KT")
            nc.vector.tensor_copy(k_nat[:, :, 0:(NW - 1) * P], ps[:, b:b + NH, 0:(NW - 1) * P]).then_inc(banks_free, 1)
            differences(6)
            take_level("Ld", DIAG)
            decayed(6)
            take_level("L4", 4)
            differences(7)
            decayed(7)
            b = turned_banks("KV0")
            after_own(nc.vector.tensor_copy(state[:, :, 0, :], ps[:, b:b + NH, 0:DV]))
            dve.wait_ge(glast_ready, 1)
            for h in range(NH):
                m = nc.vector.scalar_tensor_tensor(out=state[:, h, 1, :], in0=state[:, h, 0, :],
                                                   scalar=glast[:, h, 1:2], in1=ps[:, b + h, DV:2 * DV],
                                                   op0=ALU.mult, op1=ALU.add)
            m.then_inc(banks_free, 1)
            dve.wait_ge(banks_free, INDEX["KV0"] + 1)
            b = turned_banks("KV1")
            for h in range(NH):
                m = nc.vector.scalar_tensor_tensor(out=state[:, h, 2, :], in0=state[:, h, 1, :],
                                                   scalar=glast[:, h, 2:3], in1=ps[:, b + h, 0:DV],
                                                   op0=ALU.mult, op1=ALU.add)
            m.then_inc(banks_free, 1)
            take_level("L5", 5)
            differences(8)
            decayed(8)
            take_level("L6", 6)
            for part in range(2):
                b = turned_banks(f"o{part}")
                for j in range(4):
                    nc.vector.tensor_copy(o_T[part][:, j, :], ps[:, b + j, :]).then_inc(o_ready, 1)
                dve.wait_ge(o_ready, 4 * part + 4)
                dve.sem_inc(banks_free, 1)
            for h in range(NH):
                sq = o_sq[h // 2]
                dve.wait_ge(osq_ready, 2 * h + 2)
                nc.vector.tensor_tensor(sq[:, 2 * (h % 2), :], sq[:, 2 * (h % 2), :], sq[:, 2 * (h % 2) + 1, :],
                                        ALU.add).then_inc(opair_ready, 1)
            b = turned_banks("osum")
            dve.wait_ge(oroot_ready, NH)
            dve.sem_inc(banks_free, 1)
            after_own(nc.vector.reciprocal(rstd_o, rstd_o))
            for t in range(ND):
                m = nc.vector.tensor_tensor(o_T[t // 4][:, t % 4, :], o_T[t // 4][:, t % 4, :], rstd_o[:, t // 2, :],
                                            ALU.mult)
            after_own(m)

            def gated(part):
                for j in range(4):
                    t = 4 * part + j
                    o = o_T[part][:, j, :]
                    nc.vector.scalar_tensor_tensor(out=o, in0=o, scalar=vec[:, GN_G + t:GN_G + t + 1],
                                                   in1=gate_T[part][:, j, :], op0=ALU.mult,
                                                   op1=ALU.mult).then_inc(y_ready, 1)
                for j in range(4):
                    lower_y(4 * part + j, o_T[part][:, j, :])

            gated(0)
            splits_put_off()
            gate(1)
            dve.wait_ge(fn_ready, pre.n)
            dve.sem_inc(banks_free, 1)
            gated(1)
            splits_put_off()
            drain_out(NU, FFN1)

            swiglu(FINAL)
            finish_norm()
            for tile in range(ND):
                nc.vector.scalar_tensor_tensor(out=result[:, tile, :], in0=xT[:, tile, :],
                                               scalar=vec[:, GAIN + FINAL * ND + tile:GAIN + FINAL * ND + tile + 1],
                                               in1=rstd_row[:], op0=ALU.mult, op1=ALU.mult).then_inc(out_ready, 1)


ITEMS = [64, 32, 16, 8, "end", 4, 2, 1, "start"]


def _tiles(w, col, width):
    return [w[k * P:(k + UK) * P, col:col + width].reshape(UK, P, width) for k in range(0, w.shape[0], UK)]


def _weight_stream(np, a_w_in, a_w_out, b_w_in, b_w_out, gate, up, down):
    units = []

    def one(w, col, k0=0, nk=None):
        nk = w.shape[0] // P if nk is None else nk
        for k in range(k0, k0 + nk, UK):
            units.append(w[k * P:(k + UK) * P, col:col + UC].reshape(UK, P, UC).transpose(1, 0, 2))

    def swiglu(g, u, d):
        for s in range(11):
            for k in range(0, ND, UK):
                both = [w[k * P:(k + UK) * P, s * 256:(s + 1) * 256].reshape(UK, P, 256) for w in (g, u)]
                units.append(np.concatenate(both, axis=2).transpose(1, 0, 2))
            if s in (3, 7):
                for half in range(2):
                    one(d, half * UC, (s - 3) * 2, GROUP)
        for half in range(2):
            one(d, half * UC, 2 * GROUP, LAST)

    for s in range(6):
        one(a_w_in, SGW + s * UC)
    for g in range(NC_SG // GROUP):
        one(a_w_in, 2 * g * UC)
        one(a_w_in, (2 * g + 1) * UC)
        for half in range(2):
            one(a_w_out, half * UC, g * GROUP, GROUP)
    swiglu(gate[0], up[0], down[0])
    low_rank = np.zeros((D, UC), b_w_in.dtype)
    low_rank[:, 0:RANK] = b_w_in[:, 6 * UC:6 * UC + RANK]
    one(low_rank, 0)
    for s in (0, 1, 2, 3, 4, 5):
        one(b_w_in, s * UC)
    for half in range(2):
        one(b_w_out, half * UC)
    swiglu(gate[1], up[1], down[1])
    assert len(units) == UNITS
    return np.stack(units).reshape(UNITS, P, UK * UC)


def kernel(**inputs):
    import numpy as np
    import concourse.bacc as bacc
    from concourse.bass_utils import run_bass_kernel_spmd

    a = {n: np.asarray(v) for n, v in inputs.items()}
    columns = [np.stack([a["mix_norm"][0], a["ffn_norm"][0], a["mix_norm"][1], a["ffn_norm"][1],
                         a["final_norm"]]).reshape(5 * ND, P),
               a["a_ln_g"].reshape(-1, P), a["a_ln_b"].reshape(-1, P), a["b_b_g"].reshape(-1, P),
               a["b_gn_g"].reshape(-1, P)]
    at = np.arange(P)
    key, query = at[:, None], at[None, :]
    level_masks = [(key // (2 * m) == query // (2 * m)) & (key % (2 * m) < m) & (query % (2 * m) >= m)
                   for m in LEVELS] + [key == query]
    arrays = {
        "x_T": a["x"][0].T.reshape(ND, P, T).transpose(1, 0, 2),
        "weights": _weight_stream(np, a["a_w_in"][0], a["a_w_out"][0], a["b_w_in"][0], a["b_w_out"][0],
                                  a["ffn_w_gate"], a["ffn_w_up"], a["ffn_w_down"]),
        "spatial_T": a["a_w_s"][0].transpose(2, 0, 1),
        "spatial_bias": a["a_b_s"][0],
        "vectors": np.concatenate(columns).T,
        "w_g2": a["b_w_g2"][0],
        "level_masks": np.stack(level_masks, axis=1).astype(np.float32),
        "identity": np.eye(P, dtype=np.float32),
    }
    arrays = {n: np.ascontiguousarray(v) for n, v in arrays.items()}
    nc = bacc.Bacc("TRN2", target_bir_lowering=False, num_devices=1)
    args = {n: nc.dram_tensor(n, v.shape, mybir.dt.from_np(v.dtype), kind="ExternalInput").ap()
            for n, v in arrays.items()}
    out_T = nc.dram_tensor("out_T", (D, T), F32, kind="ExternalOutput").ap()
    build_trunk(nc, out_T=out_T, **args)
    run = run_bass_kernel_spmd(nc, [arrays], core_ids=[0])
    return np.ascontiguousarray(run.results[0]["out_T"].T)[None]
```

```python
from contextlib import ExitStack, contextmanager

import concourse.bass as bass
from concourse import mybir

ALU = mybir.AluOpType
ACT = mybir.ActivationFunctionType
F32 = mybir.dt.float32
F32R = mybir.dt.float32r
U8 = mybir.dt.uint8

P = 128
T = 512
NW = T // P
D = 1024
ND = D // P
CH = 64
SGW = 3 * D
NG = 8
NC_SG = SGW // P
CT_G = NC_SG // NG
NH = 4
DV = D // NH
DK = D // 2 // NH
RANK = 16
TAU = 16.0
HID = 2816
EPS = 1e-6

UK = 2
UC = 512
RING = 4
LEAD = 7
GROUP = 8
LAST = HID // P - 2 * GROUP
NU = ND // UK

LEVELS = [64, 32, 16, 8, 4, 2, 1]
DIAG = len(LEVELS)
MIX0, FFN0, MIX1, FFN1, FINAL = range(5)
GAIN, LN_G, LN_B, GATE_B, GN_G, N_VEC = 0, 40, 64, 88, 92, 100

UNITS = (6 * NU
         + NC_SG // GROUP * (2 * NU + 2 * GROUP // UK)
         + 2 * (11 * NU + 2 * (HID // P) // UK)
         + 7 * NU + 2 * NU)

SETS = []
for _s in range(6):
    SETS.append((f"v{_s}", NU))
for _g in range(3):
    SETS += [(f"u{_g}0", NU), (f"s{_g}0", 0), (f"u{_g}1", NU), (f"s{_g}1", 0),
             (f"so{_g}0", NU), (f"so{_g}1", NU)]


def _swiglu_sets(f):
    for s in range(11):
        SETS.append((f"{f}g{s}", NU))
        if s in (3, 7):
            SETS.extend([(f"{f}o{s}0", NU), (f"{f}o{s}1", NU)])
    SETS.extend([(f"{f}oz0", LAST // UK), (f"{f}oz1", LAST // UK)])


_swiglu_sets("f")
SETS += [("q", NU), ("gz", NU), ("z", 0), ("k", NU), ("gv0", NU), ("L0", 0), ("L1", 0), ("L2", 0), ("gv1", NU),
         ("L3", 0), ("KT", 0), ("L4", 0), ("KV0", 0), ("KV1", 0), ("Ld", 0), ("r0", NU),
         ("L5", 0), ("L6", 0), ("o0", 0), ("o1", 0), ("osum", 0), ("r1", NU), ("go0", NU), ("go1", NU)]
_swiglu_sets("F")
SETS.append(("end", 0))
ROWSUMS = 1
INDEX = {name: n + ROWSUMS for n, (name, _) in enumerate(SETS)}


def bank(name):
    return 4 * (INDEX[name] % 2)


def units_through(name):
    return sum(n for _, n in SETS[:INDEX[name] - ROWSUMS + 1])


def turned_through(name):
    return ROWSUMS + sum(n == 0 for _, n in SETS[:INDEX[name] - ROWSUMS + 1]) + (name in ("osum", "end"))


class Count:

    def __init__(self, n=0):
        self.n, self.i, self.per = n, None, 0

    def add(self, k=1):
        self.n += k
        return self.value()

    def value(self, more=0):
        return self.n + more if self.i is None else self.i * self.per + (self.n + more)


@contextmanager
def turns(eng, times, *counts):
    before = [c.n for c, _ in counts]
    with eng.Fori(0, times) as i:
        for c, per in counts:
            c.i, c.per = i, per
        yield i
    for (c, per), n in zip(counts, before):
        assert c.n == n + per, "a count grew by another amount than stated"
        c.i, c.n = None, n + per * times


def build_trunk(nc, x_T, weights, spatial_T, spatial_bias, vectors, w_g2, level_masks, identity, out_T):
    with ExitStack() as ctx:
        top = [(nc.sbuf_base + 31) // 32 * 32]

        def place(name, shape, dt=F32, over=None):
            at = top[0] if over is None else over
            words = 1
            for s in shape[1:]:
                words *= s
            if over is None:
                top[0] = at + (words * (1 if dt == U8 else 4) + 31) // 32 * 32
            t = nc.alloc_sbuf_tensor_at(name, shape, dt, offset=at)
            return t, at

        xT, _ = place("xT", [P, ND, T])
        h_hi, _ = place("h_hi", [P, ND, T], F32R)
        h_lo, _ = place("h_lo", [P, ND, T], F32R)
        y_hi, at_yhi = place("y_hi", [P, GROUP, T], F32R)
        y_lo, at_ylo = place("y_lo", [P, GROUP, T], F32R)
        raw, _ = place("raw", [P, RING, UK * UC])
        w_hi, _ = place("w_hi", [P, RING, UK * UC], F32R)
        w_lo, _ = place("w_lo", [P, RING, UK * UC], F32R)
        arena, _ = place("arena", [P, 17 * 1024])
        sumsq, _ = place("sumsq", [P, T])
        square, _ = place("square", [P, 2, T])
        rstd_row, _ = place("rstd_row", [P, T])
        ident, _ = place("ident", [P, P])
        ones, _ = place("ones", [P, P])
        masks, _ = place("masks", [P, DIAG + 1, P], U8)
        vec, _ = place("vec", [P, N_VEC])
        rstd_col, _ = place("rstd_col", [P, NW])
        eps, _ = place("eps", [P, 1])
        stats, _ = place("stats", [P, NW, 6, 6])
        moments, _ = place("moments", [P, NW, 2])
        ln_rstd, _ = place("ln_rstd", [P, NW])
        rstd_o, _ = place("rstd_o", [P, NH * NW])
        glast, _ = place("glast", [P, NH, NW])
        state, _ = place("state", [P, NH, NW - 1, DV], over=at_yhi)
        v_gla, _ = place("v_gla", [P, NW, D], over=at_ylo)
        ps = ctx.enter_context(nc.psum_tensor("ps", [P, 8, T], F32))

        def region(at, a, b):
            return arena[:, at * 1024:at * 1024 + a * b].rearrange("p (a b) -> p a b", a=a)

        v_sg = region(0, NW, SGW)
        masks_in = region(0, DIAG + 1, P)
        ws_T = region(12, NG, P)
        ws_rows = region(13, NG, P)
        bias_s = region(14, NG, P)
        pair = region(15, 4, T)
        s_bias = square[:, 0, :].rearrange("p (j t) -> p j t", j=4)
        q_T = region(0, NH, T)
        k_T = region(2, NH, T)
        G_T = region(4, NH, T)
        qk_third, _ = place("qk_third", [P, NH, T], over=at_yhi)
        QK = [region(6, NH, T), region(8, NH, T), qk_third[:]]
        qG_T = G_T
        A_T = region(10, NH, T)
        gate_T = [region(12, NH, T), region(2, NH, T)]
        k_nat = region(14, NH, T)
        diag_o = region(14, NH * NW, P)
        g2_sb = arena[0:RANK, 16 * 1024:16 * 1024 + NH * DK]
        gz_T = arena[0:RANK, 16 * 1024 + T:17 * 1024]
        o_T = QK[0:2]
        o_sq = [q_T, G_T]
        result = region(0, ND, T)

        def sem(name):
            return ctx.enter_context(nc.semaphore(name))

        landed = [sem(f"weights_landed_{i}") for i in range(RING)]
        hi_ready = sem("hi_ready")
        lo_ready = sem("lo_ready")
        units_used = sem("units_used")
        turned = sem("turned")
        banks_free = sem("banks_free")
        x_landed = [sem(f"x_landed_{i}") for i in range(2)]
        spatial_landed = sem("spatial_landed")
        vec_landed = sem("vec_landed")
        late_landed = sem("late_landed")
        g2_landed = sem("g2_landed")
        consts_ready = sem("consts_ready")
        x_ready = sem("x_ready")
        hhi_ready = sem("hhi_ready")
        hlo_ready = sem("hlo_ready")
        sq_ready = sem("sq_ready")
        sum_ready = sem("sum_ready")
        norm_sums = sem("norm_sums")
        root_ready = sem("root_ready")
        rstd_ready = sem("rstd_ready")
        dve_own = sem("dve_own")
        act_own = sem("act_own")
        pre_ready = sem("pre_ready")
        fn_ready = sem("fn_ready")
        y_ready = sem("y_ready")
        yhi_ready = sem("yhi_ready")
        ylo_ready = sem("ylo_ready")
        v_ready = sem("v_ready")
        stats_ready = sem("stats_ready")
        var_ready = sem("var_ready")
        std_ready = sem("std_ready")
        vhat_ready = sem("vhat_ready")
        softplus_ready = sem("softplus_ready")
        diff_ready = sem("diff_ready")
        exp_ready = sem("exp_ready")
        qk_ready = sem("qk_ready")
        glast_ready = sem("glast_ready")
        o_ready = sem("o_ready")
        osq_ready = sem("osq_ready")
        ocopy_ready = sem("ocopy_ready")
        oroot_ready = sem("oroot_ready")
        diag_ready = sem("diag_ready")
        out_ready = sem("out_ready")
        out_stored = sem("out_stored")

        block = ctx.enter_context(nc.Block())

        @block.sync
        def _(sp):
            for half in range(2):
                sp.dma_start(xT[:, 4 * half:4 * half + 4, :], x_T[:, 4 * half:4 * half + 4, :]).then_inc(
                    x_landed[half], 16)
                sp.dma_start(raw[:, half, :], weights[half]).then_inc(landed[half], 16)
            for slot in range(2, RING):
                sp.dma_start(raw[:, slot, :], weights[slot]).then_inc(landed[slot], 16)
            issued = Count(RING)
            with turns(sp, UNITS // RING - 1, (issued, RING)) as i:
                for slot in range(RING):
                    sp.wait_ge(lo_ready, issued.value(1 - RING))
                    sp.dma_start(raw[:, slot, :], weights[bass.ds(i * RING + (RING + slot), 1), :, :].rearrange(
                        "u p c -> p (u c)")).then_inc(landed[slot], 16)
                    issued.add()
            for tile in range(ND):
                sp.wait_ge(out_ready, tile + 1)
                sp.dma_start(out_T[tile * P:(tile + 1) * P, :], result[:, tile, :]).then_inc(out_stored, 16)
            sp.wait_ge(out_stored, 16 * ND)

        @block.gpsimd
        def _(pool):
            pool.dma_start(ws_T[0:CH], spatial_T[0:CH]).then_inc(spatial_landed, 16)
            pool.dma_start(ws_T[CH:P, :, CH:P], spatial_T[CH:P, :, CH:P]).then_inc(spatial_landed, 16)
            pool.dma_start(bias_s, spatial_bias.partition_broadcast(P)).then_inc(late_landed, 16)
            pool.dma_start(masks_in, level_masks).then_inc(late_landed, 16)
            pool.dma_start(ident[:], identity).then_inc(late_landed, 16)
            nc.gpsimd.memset(ones[:], 1.0).then_inc(consts_ready, 1)
            pool.wait_ge(consts_ready, 1)
            nc.gpsimd.memset(eps[:], EPS).then_inc(consts_ready, 1)
            pool.wait_ge(consts_ready, 2)
            nc.gpsimd.memset(ws_T[CH:P, :, 0:CH], 0.0).then_inc(consts_ready, 1)
            pool.wait_ge(consts_ready, 3)
            for n in range(5 * ND):
                if n == ND:
                    pool.wait_ge(late_landed, 48)
                    nc.gpsimd.tensor_copy(masks[:], masks_in).then_inc(consts_ready, 1)
                pool.wait_ge(sq_ready, n + 1)
                if n % ND == 0:
                    nc.gpsimd.tensor_copy(sumsq[:], square[:, 0, :]).then_inc(sum_ready, 1)
                else:
                    pool.wait_ge(sum_ready, n)
                    nc.gpsimd.tensor_tensor(sumsq[:], sumsq[:], square[:, n % 2, :], ALU.add).then_inc(sum_ready, 1)

        @block.tensor
        def _(pe):
            used = Count()
            sets = Count()
            y_seen = Count()
            norms = Count()
            h_before = Count()

            def open_set():
                b = 4 * (sets.n % 2)
                if sets.i is not None or sets.n >= 2:
                    pe.wait_ge(banks_free, sets.value(-1))
                sets.add()
                return b

            def three_passes(acc, w_h, w_l, o_h, o_l, weights_stationary, start, stop):
                if weights_stationary:
                    nc.tensor.matmul(acc, w_h, o_l, start=start, stop=False)
                    nc.tensor.matmul(acc, w_h, o_h, start=False, stop=False)
                    return nc.tensor.matmul(acc, w_l, o_h, start=False, stop=stop)
                nc.tensor.matmul(acc, o_h, w_l, start=start, stop=False)
                nc.tensor.matmul(acc, o_h, w_h, start=False, stop=False)
                return nc.tensor.matmul(acc, o_l, w_h, start=False, stop=stop)

            def norm_matmuls(b):
                pe.wait_ge(sum_ready, norms.add() * ND)
                nc.tensor.matmul(ps[:, b + 3, :], ones[:], sumsq[:], start=True, stop=True)
                for w in range(NW):
                    m = nc.tensor.matmul(ps[:, b + 2, w:w + 1], sumsq[:, w * P:(w + 1) * P], ones[:, 0:1],
                                         start=True, stop=True)
                m.then_inc(norm_sums, 1)

            def product_set(hi, lo, nk, natural=False, tiles=4, wait_h=False, wait_y=False,
                            norm_inside=False, norm_before=False, inside=None, late_inside=None):
                b = open_set()
                for k in range(0, nk, UK):
                    pe.wait_ge(lo_ready, used.value(1))
                    if wait_h:
                        pe.wait_ge(hlo_ready, h_before.n + k + UK)
                    if wait_y:
                        pe.wait_ge(ylo_ready, y_seen.value(k + UK))
                    if inside is not None and k == UK:
                        inside()
                    if late_inside is not None and k == nk - UK:
                        late_inside()
                    slot = used.n % RING
                    for t in range(tiles):
                        if norm_before and k == 0 and t == 2:
                            pe.wait_ge(root_ready, norms.n)
                        if norm_inside and k == nk - UK and t == 0:
                            pe.wait_ge(banks_free, sets.n - 1)
                            norm_matmuls(4 - b)
                        for j in range(UK):
                            start, stop = k + j == 0, k + j == nk - 1
                            if natural:
                                c, o = slice(j * UC, (j + 1) * UC), slice(t * P, (t + 1) * P)
                            else:
                                c, o = slice(j * UC + t * P, j * UC + (t + 1) * P), slice(0, T)
                            m = three_passes(ps[:, b + t, :], w_hi[:, slot, c], w_lo[:, slot, c],
                                             hi[:, k + j, o], lo[:, k + j, o], not natural, start, stop)
                    m.then_inc(units_used, 1)
                    used.add()

            def in_set(**kw):
                product_set(h_hi, h_lo, ND, **kw)

            def out_sets(nk):
                for _ in range(2):
                    product_set(y_hi, y_lo, nk, wait_y=True)
                y_seen.add(nk)

            b = open_set()
            pe.wait_ge(spatial_landed, 32)
            pe.wait_ge(consts_ready, 3)
            for n in range(2):
                m = nc.tensor.matmul(ps[:, b + n, :], ones[:], ws_T[:, 4 * n:4 * n + 4, :], start=True, stop=True)
            m.then_inc(turned, 1)

            in_set(natural=True, wait_h=True, norm_inside=True)
            in_set(natural=True, norm_before=True)
            with turns(pe, 2, (used, 2 * NU), (sets, 2)):
                in_set(natural=True)
                in_set(natural=True)
            for g in range(NC_SG // GROUP):
                for s in range(2):
                    in_set()
                    b = open_set()
                    pe.wait_ge(vhat_ready, NW)
                    for j in range(4):
                        c = g * GROUP + 4 * s + j
                        for w in range(NW):
                            m = nc.tensor.matmul(ps[:, b + j, w * P:(w + 1) * P], v_sg[:, w, c * P:(c + 1) * P],
                                                 ws_T[:, c // CT_G, :], start=True, stop=True)
                    m.then_inc(turned, 1)
                out_sets(GROUP)

            def swiglu():
                h_before.add(ND)
                in_set(wait_h=True, norm_inside=True)
                in_set(norm_before=True)
                in_set()
                in_set()
                out_sets(GROUP)
                for _ in range(4):
                    in_set()
                out_sets(GROUP)
                for _ in range(3):
                    in_set()
                out_sets(LAST)

            swiglu()

            h_before.add(ND)
            in_set(wait_h=True, norm_inside=True)
            in_set(tiles=1)
            z_bank = open_set()

            def gate_logits():
                pe.wait_ge(banks_free, INDEX["gz"] + 1)
                pe.wait_ge(g2_landed, 16)
                for h in range(NH):
                    m = nc.tensor.matmul(ps[:, z_bank + h, :], g2_sb[:, h * P:(h + 1) * P], gz_T, start=True,
                                         stop=True)
                m.then_inc(turned, 1)

            in_set(norm_before=True, inside=gate_logits)

            def level(item):
                b = open_set()
                pe.wait_ge(qk_ready, item + 1)
                qk = QK[item % 3]
                for h in range(NH):
                    for w in range(NW):
                        c = slice(w * P, (w + 1) * P)
                        late = qk[:, h, c].rearrange("p (n s) -> p n s", s=2 * ITEMS[item])[:, :, ITEMS[item]:]
                        m = nc.tensor.matmul(ps[:, b + h, w * P:w * P + P // 2], qk[:, h, c], late,
                                             start=True, stop=True)
                m.then_inc(turned, 1)

            in_set(natural=True)
            level(0)
            level(1)
            level(2)
            in_set(natural=True)
            level(3)
            b = open_set()
            pe.wait_ge(qk_ready, 5)
            pe.wait_ge(late_landed, 48)
            for h in range(NH):
                for w in range(NW - 1):
                    c = slice(w * P, (w + 1) * P)
                    m = nc.tensor.transpose(ps[:, b + h, c], QK[1][:, h, c], ident[:])
            m.then_inc(turned, 1)
            level(5)
            for part, windows in enumerate(((0, 1), (2,))):
                b = open_set()
                pe.wait_ge(banks_free, INDEX["KT"] + 1)
                pe.wait_ge(v_ready, 8 * NW)
                for h in range(NH):
                    for n, w in enumerate(windows):
                        m = nc.tensor.matmul(ps[:, b + h, n * DV:(n + 1) * DV], k_nat[:, h, w * P:(w + 1) * P],
                                             v_gla[:, w, h * DV:(h + 1) * DV], start=True, stop=True)
                m.then_inc(turned, 1)
            b = open_set()
            for h in range(NH):
                for w in range(NW):
                    c = slice(w * P, (w + 1) * P)
                    m = nc.tensor.matmul(ps[:, b + h, c], k_T[:, h, c], q_T[:, h, c], start=True, stop=True)
            m.then_inc(turned, 1)
            in_set()
            level(6)
            level(7)
            for part in range(2):
                b = open_set()
                pe.wait_ge(banks_free, INDEX["L6"] + 1)
                pe.wait_ge(banks_free, INDEX["KV1"] + 1)
                pe.wait_ge(qk_ready, 9)
                for j in range(4):
                    h, v0 = 2 * part + j // 2, j % 2 * P
                    for w in range(NW):
                        c = slice(w * P, (w + 1) * P)
                        m = nc.tensor.matmul(ps[:, b + j, c], v_gla[:, w, h * DV + v0:h * DV + v0 + P], A_T[:, h, c],
                                             start=True, stop=w == 0)
                        if w:
                            m = nc.tensor.matmul(ps[:, b + j, c], state[:, h, w - 1, v0:v0 + P], qG_T[:, h, c],
                                                 start=False, stop=True)
                m.then_inc(turned, 1)
            o_bank = open_set()

            def head_sums():
                pe.wait_ge(osq_ready, ND)
                for h in range(NH):
                    for w in range(NW):
                        n = h * NW + w
                        for half in range(2):
                            m = nc.tensor.matmul(ps[:, o_bank + 3, n:n + 1],
                                                 o_sq[h // 2][:, 2 * (h % 2) + half, w * P:(w + 1) * P],
                                                 ones[:, 0:1], start=half == 0, stop=half == 1)
                m.then_inc(turned, 1)

            def spread_rstd():
                pe.wait_ge(diag_ready, 1)
                for h in range(NH):
                    for w in range(NW):
                        m = nc.tensor.matmul(ps[:, o_bank + h, w * P:(w + 1) * P], ones[:],
                                             diag_o[:, h * NW + w, :], start=True, stop=True)
                m.then_inc(turned, 1)

            in_set(inside=head_sums, late_inside=spread_rstd)
            out_sets(ND)

            swiglu()
            b = open_set()
            norm_matmuls(b)

        @block.scalar
        def _(act):
            unit = Count()
            x_seen, pre, y_seen, norms, squares, diffs = (Count() for _ in range(6))

            def split():
                if unit.i is None and unit.n >= UNITS:
                    return
                slot, rounds = unit.n % RING, 16 * (unit.n // RING + 1)
                act.wait_ge(landed[slot], rounds if unit.i is None else unit.i * (16 * unit.per // RING) + rounds)
                if unit.i is not None or unit.n >= RING:
                    act.wait_ge(units_used, unit.value(1 - RING))
                nc.scalar.copy(w_hi[:, slot, :], raw[:, slot, :]).then_inc(hi_ready, 1)
                unit.add()

            def drain(n, piece=None):
                if piece is not None:
                    for j in range(4):
                        piece(j)
                for _ in range(n):
                    split()

            def finish_norm(b):
                act.wait_ge(norm_sums, norms.add())
                nc.scalar.activation(rstd_col[:], ps[:, b + 2, 0:NW], ACT.Sqrt, bias=eps[:, 0:1], scale=1.0 / D)
                nc.scalar.activation(rstd_row[:], ps[:, b + 3, :], ACT.Sqrt, bias=eps[:, 0:1],
                                     scale=1.0 / D).then_inc(root_ready, 1)

            def square_tile(tile):
                if squares.n > 1:
                    act.wait_ge(sum_ready, squares.n - 1)
                nc.scalar.activation(square[:, squares.n % 2, :], xT[:, tile, :], ACT.Square).then_inc(sq_ready, 1)
                squares.add()

            def upper_h(tile, gain):
                nc.scalar.activation(h_hi[:, tile, :], xT[:, tile, :], ACT.Copy,
                                     scale=vec[:, GAIN + gain * ND + tile:GAIN + gain * ND + tile + 1]).then_inc(
                                         hhi_ready, 1)

            def drain_out(n, gain):
                for half in range(2):
                    def piece(j):
                        if gain is None:
                            x_seen.add()
                            return
                        act.wait_ge(x_ready, x_seen.add())
                        if gain == FINAL:
                            square_tile(4 * half + j)
                        else:
                            upper_h(4 * half + j, gain)
                            square_tile(4 * half + j)
                    drain(n, piece)

            def upper_y(tile, source):
                act.wait_ge(y_ready, y_seen.add())
                nc.scalar.copy(y_hi[:, tile, :], source).then_inc(yhi_ready, 1)

            def function(tile, f):
                act.wait_ge(pre_ready, pre.add())
                nc.scalar.activation(tile, tile, f).then_inc(fn_ready, 1)

            act.dma_start(vec[:], vectors).then_inc(vec_landed, 16)
            act.wait_ge(vec_landed, 16)
            act.wait_ge(consts_ready, 3)
            for tile in range(ND):
                if tile % 4 == 0:
                    act.wait_ge(x_landed[tile // 4], 16)
                upper_h(tile, MIX0)
                if tile % 2:
                    split()
            for tile in range(ND):
                square_tile(tile)
            drain(LEAD - ND // 2)

            finish_norm(bank("v1"))
            act.wait_ge(rstd_ready, norms.n)
            act.wait_ge(consts_ready, 4)

            def v_set(s, col):
                split()
                for w in range(NW):
                    nc.scalar.activation(v_sg[:, w, bass.ds(col, UC)], ps[:, bank(f"v{s}") + w, :], ACT.Gelu,
                                         scale=rstd_col[:, w:w + 1]).then_inc(v_ready, 1)

            with turns(act, 2, (unit, 2 * NU)) as i:
                for s in range(2):
                    v_set(s, i * (2 * UC) + s * UC)
                    drain(NU - 1)
            v_set(4, 4 * UC)
            drain(NU - 1)
            v_set(5, 5 * UC)
            act.wait_ge(var_ready, 1)
            nc.scalar.activation(ln_rstd[:], moments[:, :, 1], ACT.Sqrt, bias=eps[:, 0:1]).then_inc(std_ready, 1)
            drain(NU - 1)

            for g in range(NC_SG // GROUP):
                for s in range(2):
                    for j in range(4):
                        function(pair[:, j, :], ACT.Gelu)
                    split()
                    for j in range(4):
                        upper_y(4 * s + j, pair[:, j, :])
                    drain(NU - 1)
                drain_out(GROUP // UK, FFN0 if g == 2 else None)

            def gate_up(tile0):
                for j in range(2):
                    function(pair[:, j, :], ACT.Silu)
                split()
                for j in range(2):
                    upper_y(tile0 + j, pair[:, j, :])
                drain(NU - 1)

            def swiglu(f, gain):
                finish_norm(bank(f + "g1"))
                gate_up(0)
                with turns(act, 2, (unit, 24), (pre, 8), (y_seen, 8), (x_seen, ND)):
                    for s in range(1, 4):
                        gate_up(2 * s)
                    drain_out(GROUP // UK, None)
                    gate_up(0)
                for s in range(1, 3):
                    gate_up(2 * s)
                drain_out(LAST // UK, gain)

            swiglu("f", MIX1)

            act.wait_ge(ylo_ready, y_seen.n)
            act.dma_start(g2_sb, w_g2).then_inc(g2_landed, 16)
            finish_norm(bank("gz"))
            drain(NU)
            drain(1)
            act.wait_ge(banks_free, INDEX["z"] + 1)
            nc.scalar.activation(QK[0], G_T, ACT.Abs).then_inc(act_own, 1)
            act.wait_ge(act_own, 1)
            nc.scalar.activation(QK[0], QK[0], ACT.Exp, scale=-1.0).then_inc(act_own, 1)
            act.wait_ge(act_own, 2)
            nc.scalar.activation(QK[0], QK[0], ACT.Ln, bias=ones[:, 0:1]).then_inc(softplus_ready, 1)
            drain(NU - 1)

            def exponential():
                buf = QK[diffs.n % 3]
                act.wait_ge(diff_ready, diffs.add())
                nc.scalar.activation(buf, buf, ACT.Exp, scale=1.0 / TAU).then_inc(exp_ready, 1)

            for _ in range(3):
                exponential()
            nc.scalar.activation(glast[:], G_T[:, :, P - 1::P], ACT.Exp, scale=1.0 / TAU).then_inc(glast_ready, 1)
            drain(NU)

            def v_pieces(half):
                name = f"gv{half}"
                act.wait_ge(units_used, units_through(name))
                for w in range(NW):
                    nc.scalar.activation(v_gla[:, w, half * UC:(half + 1) * UC], ps[:, bank(name) + w, :], ACT.Copy,
                                         scale=rstd_col[:, w:w + 1]).then_inc(v_ready, 1)
                split()

            v_pieces(0)
            for _ in range(3):
                exponential()
            drain(NU - 1)
            v_pieces(1)
            for _ in range(2):
                exponential()
            act.wait_ge(diff_ready, 8)
            act.wait_ge(glast_ready, 1)
            nc.scalar.activation(G_T, G_T, ACT.Exp, scale=1.0 / TAU).then_inc(exp_ready, 1)
            drain(NU - 1)
            drain(1, lambda j: function(gate_T[0][:, j, :], ACT.Silu))
            for part in range(2):
                act.wait_ge(turned, turned_through(f"o{part}"))
                for j in (2, 3):
                    nc.scalar.copy(o_T[part][:, j, :], ps[:, bank(f"o{part}") + j, :]).then_inc(ocopy_ready, 1)
                act.wait_ge(ocopy_ready, 2 * part + 2)
                act.wait_ge(o_ready, 2 * part + 2)
                for j in range(4):
                    nc.scalar.activation(o_sq[part][:, j, :], o_T[part][:, j, :], ACT.Square).then_inc(osq_ready, 1)
            act.wait_ge(turned, turned_through("osum") - 1)
            nc.scalar.activation(rstd_o[:], ps[:, bank("osum") + 3, 0:NH * NW], ACT.Sqrt, bias=eps[:, 0:1],
                                 scale=1.0 / DV).then_inc(oroot_ready, 1)
            for t in range(4):
                upper_y(t, o_T[0][:, t, :])
            drain(NU - 1)
            for j in range(4):
                function(gate_T[1][:, j, :], ACT.Silu)
            for t in range(4):
                upper_y(4 + t, o_T[1][:, t, :])
            drain(NU)
            drain_out(NU, FFN1)

            swiglu("F", FINAL)
            finish_norm(bank("end"))

        @block.vector
        def _(dve):
            unit = Count()
            drained = Count()
            sets = Count()
            x_done, h_done, pre, y_done, norms, v_seen, own, y_made = (Count() for _ in range(8))

            def split():
                if unit.i is None and unit.n >= UNITS:
                    return
                slot = unit.n % RING
                dve.wait_ge(hi_ready, unit.value(1))
                nc.vector.tensor_tensor(w_lo[:, slot, :], raw[:, slot, :], w_hi[:, slot, :].bitcast(F32),
                                        ALU.subtract).then_inc(lo_ready, 1)
                unit.add()

            def splits(n):
                for _ in range(n):
                    split()

            def product_banks(n):
                b = 4 * (sets.n % 2)
                dve.wait_ge(units_used, drained.add(n))
                sets.add()
                return b

            def turned_banks(name):
                b = 4 * (sets.n % 2)
                assert sets.i is not None or sets.n == INDEX[name]
                dve.wait_ge(turned, turned_through(name))
                sets.add()
                return b

            def after_own(ins):
                ins.then_inc(dve_own, 1)
                dve.wait_ge(dve_own, own.add())

            def finish_norm():
                dve.wait_ge(root_ready, norms.add())
                nc.vector.reciprocal(rstd_col[:], rstd_col[:])
                nc.vector.reciprocal(rstd_row[:], rstd_row[:]).then_inc(rstd_ready, 1)
                dve.wait_ge(rstd_ready, norms.n)

            def lower_h(tile, gain):
                dve.wait_ge(hhi_ready, h_done.add())
                nc.vector.scalar_tensor_tensor(out=h_lo[:, tile, :], in0=xT[:, tile, :],
                                               scalar=vec[:, GAIN + gain * ND + tile:GAIN + gain * ND + tile + 1],
                                               in1=h_hi[:, tile, :].bitcast(F32), op0=ALU.mult,
                                               op1=ALU.subtract).then_inc(hlo_ready, 1)

            def drain_out(n, gain):
                for half in range(2):
                    b = product_banks(n)
                    for j in range(4):
                        tile = 4 * half + j
                        nc.vector.tensor_tensor(xT[:, tile, :], ps[:, b + j, :], xT[:, tile, :], ALU.add).then_inc(
                            x_ready, 1)
                        x_done.add()
                        if gain not in (None, FINAL) and j > 0:
                            lower_h(tile - 1, gain)
                    dve.wait_ge(x_ready, x_done.value())
                    dve.sem_inc(banks_free, 1)
                    if gain not in (None, FINAL):
                        lower_h(4 * half + 3, gain)
                    splits(n)

            def lower_y(tile, source):
                dve.wait_ge(yhi_ready, y_done.add())
                nc.vector.tensor_tensor(y_lo[:, tile, :], source, y_hi[:, tile, :].bitcast(F32),
                                        ALU.subtract).then_inc(ylo_ready, 1)

            dve.wait_ge(vec_landed, 16)
            dve.wait_ge(x_landed[0], 16)
            for tile in range(ND):
                if tile == 4:
                    dve.wait_ge(x_landed[1], 16)
                lower_h(tile, MIX0)
                if tile % 2:
                    split()
            b = 4 * (sets.n % 2)
            dve.wait_ge(turned, 1)
            nc.vector.tensor_copy(ws_rows.rearrange("p g t -> p (g t)"),
                                  ps[:, b:b + 2, :].rearrange("p a t -> p (a t)")).then_inc(banks_free, 1)
            sets.add()
            splits(LEAD - ND // 2)

            finish_norm()

            def v_set(n):
                dve.wait_ge(v_ready, v_seen.add(NW))
                split()
                for w in range(NW):
                    nc.vector.bn_stats(stats[:, w, bass.ds(n, 1), :].rearrange("p a s -> p (a s)"),
                                       v_sg[:, w, bass.ds(n * UC, UC)]).then_inc(stats_ready, 1)
                dve.sem_inc(banks_free, 1)
                drained.add(NU)
                sets.add()

            with turns(dve, 2, (unit, 2 * NU), (drained, 2 * NU), (sets, 2), (v_seen, 2 * NW)) as i:
                for s in range(2):
                    v_set(i * 2 + s)
                    splits(NU - 1)
            v_set(4)
            splits(NU - 1)
            v_set(5)
            dve.wait_ge(stats_ready, 6 * NW)
            for w in range(NW):
                m = nc.vector.bn_aggr(moments[:, w, :], stats[:, w, :, :].rearrange("p a s -> p (a s)"))
            m.then_inc(var_ready, 1)
            dve.wait_ge(std_ready, 1)
            after_own(nc.vector.reciprocal(ln_rstd[:], ln_rstd[:]))
            for w in range(NW):
                nc.vector.tensor_scalar(v_sg[:, w, :], v_sg[:, w, :], moments[:, w, 0:1], ln_rstd[:, w:w + 1],
                                        ALU.subtract, ALU.mult).then_inc(vhat_ready, 1)
            splits(NU - 1)

            dve.wait_ge(late_landed, 48)
            for g in range(NC_SG // GROUP):
                for s in range(2):
                    b = product_banks(NU)
                    if y_done.n:
                        dve.wait_ge(ylo_ready, y_done.n)
                    for j in range(4):
                        nc.vector.tensor_tensor(pair[:, j, :], ps[:, b + j, :], rstd_row[:], ALU.mult).then_inc(
                            pre_ready, 1)
                        pre.add()
                    dve.wait_ge(pre_ready, pre.n)
                    dve.sem_inc(banks_free, 1)
                    split()
                    for j in range(4):
                        c = g * GROUP + 4 * s + j
                        m = nc.vector.scalar_tensor_tensor(
                            out=s_bias[:, j, :], in0=ws_rows[:, c // CT_G, :], scalar=vec[:, LN_B + c:LN_B + c + 1],
                            in1=bias_s[:, c // CT_G, :], op0=ALU.mult, op1=ALU.add)
                    after_own(m)
                    dve.wait_ge(fn_ready, pre.n)
                    b = turned_banks(f"s{g}{s}")
                    for j in range(4):
                        c = g * GROUP + 4 * s + j
                        acc = ps[:, b + j, :].rearrange("p (w t) -> p w t", w=NW)
                        m = nc.vector.scalar_tensor_tensor(
                            out=acc, in0=acc, scalar=vec[:, LN_G + c:LN_G + c + 1],
                            in1=s_bias[:, j:j + 1, :].broadcast_to([P, NW, P]), op0=ALU.mult, op1=ALU.add)
                    after_own(m)
                    for j in range(4):
                        nc.vector.tensor_tensor(pair[:, j, :], ps[:, b + j, :], pair[:, j, :], ALU.mult).then_inc(
                            y_ready, 1)
                        y_made.add()
                    dve.wait_ge(y_ready, y_made.n)
                    dve.sem_inc(banks_free, 1)
                    for j in range(4):
                        lower_y(4 * s + j, pair[:, j, :])
                    splits(NU - 1)
                drain_out(GROUP // UK, FFN0 if g == 2 else None)

            def gate_up(tile0):
                def scale(j):
                    nc.vector.tensor_tensor(pair[:, 2 + j, :], ps[:, b + 2 + j, :], rstd_row[:], ALU.mult)
                    nc.vector.tensor_tensor(pair[:, j, :], ps[:, b + j, :], rstd_row[:], ALU.mult).then_inc(
                        pre_ready, 1)
                    pre.add()

                def multiply(j):
                    dve.wait_ge(fn_ready, pre.value(j - 1))
                    nc.vector.tensor_tensor(pair[:, j, :], pair[:, j, :], pair[:, 2 + j, :], ALU.mult).then_inc(
                        y_ready, 1)

                b = product_banks(NU)
                dve.wait_ge(ylo_ready, y_done.value())
                scale(0)
                scale(1)
                multiply(0)
                multiply(1)
                dve.sem_inc(banks_free, 1)
                split()
                lower_y(tile0, pair[:, 0, :])
                lower_y(tile0 + 1, pair[:, 1, :])
                splits(NU - 1)

            def swiglu(gain):
                finish_norm()
                gate_up(0)
                with turns(dve, 2, (unit, 24), (drained, 24), (sets, 6), (pre, 8), (y_done, 8), (x_done, ND)):
                    for s in range(1, 4):
                        gate_up(2 * s)
                    drain_out(GROUP // UK, None)
                    gate_up(0)
                for s in range(1, 3):
                    gate_up(2 * s)
                drain_out(LAST // UK, gain)

            swiglu(MIX1)

            finish_norm()
            split()
            b = product_banks(NU)
            for h in range(NH):
                m = nc.vector.scalar_tensor_tensor(out=q_T[:, h, :], in0=ps[:, b + h, :], scalar=float(DK) ** -0.5,
                                                   in1=rstd_row[:], op0=ALU.mult, op1=ALU.mult)
            m.then_inc(banks_free, 1)
            splits(NU - 1)
            b = product_banks(NU)
            dve.wait_ge(g2_landed, 16)
            nc.vector.tensor_tensor(gz_T, ps[0:RANK, b, :], rstd_row[0:RANK, :], ALU.mult).then_inc(banks_free, 1)
            split()
            b = turned_banks("z")
            for h in range(NH):
                m = nc.vector.tensor_scalar(G_T[:, h, :], ps[:, b + h, :], vec[:, GATE_B + h:GATE_B + h + 1], None,
                                            ALU.add)
            m.then_inc(banks_free, 1)
            after_own(nc.vector.memset(A_T, 0.0))
            dve.wait_ge(softplus_ready, 1)
            after_own(nc.vector.scalar_tensor_tensor(out=QK[1], in0=G_T, scalar=0.0, in1=QK[0], op0=ALU.min,
                                                     op1=ALU.subtract))
            splits(NU - 1)
            for h in range(NH):
                for w in range(NW):
                    c = slice(w * P, (w + 1) * P)
                    m = nc.vector.tensor_tensor_scan(G_T[:, h, c], ones[:], QK[1][:, h, c], 0.0, ALU.mult, ALU.add)
            after_own(m)

            def halves(x, m):
                v = x.rearrange("p h (n s) -> p (h n) s", s=2 * m)
                return v[:, :, 0:m], v[:, :, m:2 * m]

            def differences(item):
                buf = QK[item % 3]
                kind = ITEMS[item]
                if kind == "end":
                    g = G_T.rearrange("p h (n s) -> p (h n) s", s=P)
                    nc.vector.tensor_tensor(buf.rearrange("p h (n s) -> p (h n) s", s=P),
                                            g[:, :, P - 1:P].broadcast_to([P, NH * NW, P]), g,
                                            ALU.subtract).then_inc(diff_ready, 1)
                else:
                    g_early, g_late = halves(G_T, kind)
                    early, late = halves(buf, kind)
                    middle = g_early[:, :, kind - 1:kind].broadcast_to([P, NH * T // (2 * kind), kind])
                    nc.vector.tensor_tensor(late, g_late, middle, ALU.subtract)
                    nc.vector.tensor_tensor(early, middle, g_early, ALU.subtract).then_inc(diff_ready, 1)

            def decayed(item):
                buf = QK[item % 3]
                kind = ITEMS[item]
                dve.wait_ge(exp_ready, item + 1)
                if kind == "end":
                    nc.vector.tensor_tensor(buf, buf, k_T, ALU.mult).then_inc(qk_ready, 1)
                else:
                    early, late = halves(buf, kind)
                    nc.vector.tensor_tensor(late, late, halves(q_T, kind)[1], ALU.mult)
                    nc.vector.tensor_tensor(early, early, halves(k_T, kind)[0], ALU.mult).then_inc(qk_ready, 1)

            def take_level(name, mask):
                dve.wait_ge(banks_free, INDEX[name])
                b = turned_banks(name)
                attn = A_T.rearrange("p h (w t) -> p (h w) t", t=P)
                acc = ps[:, b:b + NH, :].rearrange("p h (w t) -> p (h w) t", t=P)
                keep = masks[:, mask:mask + 1, :]
                if mask != DIAG:
                    m = LEVELS[mask]
                    attn = attn.rearrange("p w (n s) -> p w n s", s=2 * m)[:, :, :, m:]
                    acc = acc[:, :, 0:P // 2].rearrange("p w (n s) -> p w n s", s=m)
                    keep = keep.rearrange("p w (n s) -> p w n s", s=2 * m)[:, :, :, m:]
                    keep = keep.broadcast_to([P, NH * NW, P // (2 * m), m])
                else:
                    keep = keep.broadcast_to([P, NH * NW, P])
                nc.vector.copy_predicated(attn, keep, acc).then_inc(banks_free, 1)

            def gate(part):
                b = product_banks(NU)
                for j in range(4):
                    nc.vector.tensor_tensor(gate_T[part][:, j, :], ps[:, b + j, :], rstd_row[:], ALU.mult).then_inc(
                        pre_ready, 1)
                    pre.add()
                dve.wait_ge(pre_ready, pre.n)
                dve.sem_inc(banks_free, 1)

            def pass_v(half):
                product_banks(NU)
                dve.wait_ge(v_ready, (6 + half + 1) * NW)
                dve.sem_inc(banks_free, 1)

            for item in range(3):
                differences(item)
            b = product_banks(NU)
            for h in range(NH):
                m = nc.vector.tensor_tensor(k_T[:, h, :], ps[:, b + h, :], rstd_row[:], ALU.mult)
            m.then_inc(banks_free, 1)
            dve.wait_ge(banks_free, INDEX["k"] + 1)
            decayed(0)
            split()
            decayed(1)
            decayed(2)
            splits(NU - 1)
            pass_v(0)
            take_level("L0", 0)
            differences(3)
            take_level("L1", 1)
            differences(4)
            take_level("L2", 2)
            differences(5)
            decayed(3)
            decayed(4)
            split()
            decayed(5)
            splits(NU - 1)
            pass_v(1)
            take_level("L3", 3)
            b = turned_banks("KT")
            nc.vector.tensor_copy(k_nat[:, :, 0:(NW - 1) * P], ps[:, b:b + NH, 0:(NW - 1) * P]).then_inc(banks_free, 1)
            differences(6)
            take_level("L4", 4)
            differences(7)
            b = turned_banks("KV0")
            after_own(nc.vector.tensor_copy(state[:, :, 0, :], ps[:, b:b + NH, 0:DV]))
            dve.wait_ge(glast_ready, 1)
            for h in range(NH):
                m = nc.vector.scalar_tensor_tensor(out=state[:, h, 1, :], in0=state[:, h, 0, :],
                                                   scalar=glast[:, h, 1:2], in1=ps[:, b + h, DV:2 * DV],
                                                   op0=ALU.mult, op1=ALU.add)
            m.then_inc(banks_free, 1)
            dve.wait_ge(banks_free, INDEX["KV0"] + 1)
            b = turned_banks("KV1")
            for h in range(NH):
                m = nc.vector.scalar_tensor_tensor(out=state[:, h, 2, :], in0=state[:, h, 1, :],
                                                   scalar=glast[:, h, 2:3], in1=ps[:, b + h, 0:DV],
                                                   op0=ALU.mult, op1=ALU.add)
            m.then_inc(banks_free, 1)
            take_level("Ld", DIAG)
            split()
            decayed(6)
            decayed(7)
            dve.wait_ge(exp_ready, 9)
            nc.vector.tensor_tensor(qG_T, G_T, q_T, ALU.mult).then_inc(qk_ready, 1)
            splits(NU - 1)
            gate(0)
            split()
            take_level("L5", 5)
            take_level("L6", 6)
            for part in range(2):
                b = turned_banks(f"o{part}")
                for j in range(2):
                    nc.vector.tensor_copy(o_T[part][:, j, :], ps[:, b + j, :]).then_inc(o_ready, 1)
                dve.wait_ge(o_ready, 2 * part + 2)
                dve.wait_ge(ocopy_ready, 2 * part + 2)
                dve.sem_inc(banks_free, 1)

            def gated(t):
                o = o_T[t // 4][:, t % 4, :]
                return nc.vector.scalar_tensor_tensor(out=o, in0=o, scalar=vec[:, GN_G + t:GN_G + t + 1],
                                                      in1=gate_T[t // 4][:, t % 4, :], op0=ALU.mult, op1=ALU.mult)

            dve.wait_ge(oroot_ready, 1)
            after_own(nc.vector.reciprocal(rstd_o[:], rstd_o[:]))
            nc.vector.tensor_tensor(diag_o, ident[:].rearrange("p (n t) -> p n t", n=1).broadcast_to([P, NH * NW, P]),
                                    rstd_o[:].rearrange("p (n t) -> p n t", t=1).broadcast_to([P, NH * NW, P]),
                                    ALU.mult).then_inc(diag_ready, 1)
            for t in range(4):
                m = gated(t)
            after_own(m)
            b = turned_banks("osum")
            for t in range(ND):
                o = o_T[t // 4][:, t % 4, :]
                m = nc.vector.tensor_tensor(o, ps[:, b + t // 2, :], o, ALU.mult)
                if t < 4:
                    m.then_inc(y_ready, 1)
            after_own(m)
            dve.sem_inc(banks_free, 1)
            for t in range(4):
                lower_y(t, o_T[0][:, t, :])
            splits(NU - 1)
            gate(1)
            dve.wait_ge(fn_ready, pre.n)
            for t in range(4, ND):
                gated(t).then_inc(y_ready, 1)
            for t in range(4, ND):
                lower_y(t, o_T[1][:, t - 4, :])
            splits(NU)
            drain_out(NU, FFN1)

            swiglu(FINAL)
            finish_norm()
            for tile in range(ND):
                nc.vector.scalar_tensor_tensor(out=result[:, tile, :], in0=xT[:, tile, :],
                                               scalar=vec[:, GAIN + FINAL * ND + tile:GAIN + FINAL * ND + tile + 1],
                                               in1=rstd_row[:], op0=ALU.mult, op1=ALU.mult).then_inc(out_ready, 1)


ITEMS = [64, 32, 16, 8, "end", 4, 2, 1]


def _tiles(w, col, width):
    return [w[k * P:(k + UK) * P, col:col + width].reshape(UK, P, width) for k in range(0, w.shape[0], UK)]


def _weight_stream(np, a_w_in, a_w_out, b_w_in, b_w_out, gate, up, down):
    units = []

    def one(w, col, k0=0, nk=None):
        nk = w.shape[0] // P if nk is None else nk
        for k in range(k0, k0 + nk, UK):
            units.append(w[k * P:(k + UK) * P, col:col + UC].reshape(UK, P, UC).transpose(1, 0, 2))

    def swiglu(g, u, d):
        for s in range(11):
            for k in range(0, ND, UK):
                both = [w[k * P:(k + UK) * P, s * 256:(s + 1) * 256].reshape(UK, P, 256) for w in (g, u)]
                units.append(np.concatenate(both, axis=2).transpose(1, 0, 2))
            if s in (3, 7):
                for half in range(2):
                    one(d, half * UC, (s - 3) * 2, GROUP)
        for half in range(2):
            one(d, half * UC, 2 * GROUP, LAST)

    for s in range(6):
        one(a_w_in, SGW + s * UC)
    for g in range(NC_SG // GROUP):
        one(a_w_in, 2 * g * UC)
        one(a_w_in, (2 * g + 1) * UC)
        for half in range(2):
            one(a_w_out, half * UC, g * GROUP, GROUP)
    swiglu(gate[0], up[0], down[0])
    low_rank = np.zeros((D, UC), b_w_in.dtype)
    low_rank[:, 0:RANK] = b_w_in[:, 6 * UC:6 * UC + RANK]
    one(b_w_in, 0)
    one(low_rank, 0)
    for s in (1, 2, 3, 4, 5):
        one(b_w_in, s * UC)
    for half in range(2):
        one(b_w_out, half * UC)
    swiglu(gate[1], up[1], down[1])
    assert len(units) == UNITS
    return np.stack(units).reshape(UNITS, P, UK * UC)


def kernel(**inputs):
    import numpy as np
    import concourse.bacc as bacc
    from concourse.bass_utils import run_bass_kernel_spmd

    a = {n: np.asarray(v) for n, v in inputs.items()}
    columns = [np.stack([a["mix_norm"][0], a["ffn_norm"][0], a["mix_norm"][1], a["ffn_norm"][1],
                         a["final_norm"]]).reshape(5 * ND, P),
               a["a_ln_g"].reshape(-1, P), a["a_ln_b"].reshape(-1, P), a["b_b_g"].reshape(-1, P),
               a["b_gn_g"].reshape(-1, P)]
    at = np.arange(P)
    key, query = at[:, None], at[None, :]
    level_masks = [(key // (2 * m) == query // (2 * m)) & (key % (2 * m) < m) & (query % (2 * m) >= m)
                   for m in LEVELS] + [key == query]
    arrays = {
        "x_T": a["x"][0].T.reshape(ND, P, T).transpose(1, 0, 2),
        "weights": _weight_stream(np, a["a_w_in"][0], a["a_w_out"][0], a["b_w_in"][0], a["b_w_out"][0],
                                  a["ffn_w_gate"], a["ffn_w_up"], a["ffn_w_down"]),
        "spatial_T": a["a_w_s"][0].transpose(2, 0, 1),
        "spatial_bias": a["a_b_s"][0],
        "vectors": np.concatenate(columns).T,
        "w_g2": a["b_w_g2"][0],
        "level_masks": np.stack(level_masks, axis=1).astype(np.float32),
        "identity": np.eye(P, dtype=np.float32),
    }
    arrays = {n: np.ascontiguousarray(v) for n, v in arrays.items()}
    nc = bacc.Bacc("TRN2", target_bir_lowering=False, num_devices=1)
    args = {n: nc.dram_tensor(n, v.shape, mybir.dt.from_np(v.dtype), kind="ExternalInput").ap()
            for n, v in arrays.items()}
    out_T = nc.dram_tensor("out_T", (D, T), F32, kind="ExternalOutput").ap()
    build_trunk(nc, out_T=out_T, **args)
    run = run_bass_kernel_spmd(nc, [arrays], core_ids=[0])
    return np.ascontiguousarray(run.results[0]["out_T"].T)[None]
```

```python
from contextlib import ExitStack, contextmanager

import concourse.bass as bass
from concourse import mybir

ALU = mybir.AluOpType
ACT = mybir.ActivationFunctionType
F32 = mybir.dt.float32
F32R = mybir.dt.float32r
U8 = mybir.dt.uint8

P = 128
T = 512
NW = T // P
D = 1024
ND = D // P
CH = 64
SGW = 3 * D
NG = 8
NC_SG = SGW // P
CT_G = NC_SG // NG
NH = 4
DV = D // NH
DK = D // 2 // NH
RANK = 16
GZ_TILE = 1
TAU = 16.0
HID = 2816
EPS = 1e-6

UK = 2
UC = 512
RING = 4
LEAD = 7
GROUP = 8
LAST = HID // P - 2 * GROUP
NU = ND // UK
TURN_SETS = 4 + 2
TURN_UNITS = 4 * NU + 2 * GROUP // UK

LEVELS = [64, 32, 16, 8, 4, 2, 1]
DIAG = len(LEVELS)
ITEMS = [64, 32, 16, 8, 4, "end", 2, 1]
END = ITEMS.index("end")
MIX0, FFN0, MIX1, FFN1, FINAL = range(5)
GAIN, LN_G, LN_B, GATE_B, GN_G, N_VEC = 0, 40, 64, 88, 92, 100

UNITS = (6 * NU
         + NC_SG // GROUP * (2 * NU + 2 * GROUP // UK)
         + 2 * (11 * NU + 2 * (HID // P) // UK)
         + 7 * NU + 2 * NU)

SETS = []
for _s in range(6):
    SETS.append((f"v{_s}", NU))
for _g in range(3):
    SETS += [(f"u{_g}0", NU), (f"s{_g}0", 0), (f"u{_g}1", NU), (f"s{_g}1", 0),
             (f"so{_g}0", NU), (f"so{_g}1", NU)]


def _swiglu_sets(f):
    for s in range(11):
        SETS.append((f"{f}g{s}", NU))
        if s in (3, 7):
            SETS.extend([(f"{f}o{s}0", NU), (f"{f}o{s}1", NU)])
    SETS.extend([(f"{f}oz0", LAST // UK), (f"{f}oz1", LAST // UK)])


_swiglu_sets("f")
SETS += [("q", NU), ("gz", NU), ("z", 0), ("k", NU), ("gv0", NU), ("L0", 0), ("L1", 0), ("L2", 0), ("gv1", NU),
         ("L3", 0), ("KT", 0), ("Ld", 0), ("KV0", 0), ("L4", 0), ("KV1", 0), ("r0", NU),
         ("L5", 0), ("L6", 0), ("o0", 0), ("o1", 0), ("osum", 0), ("r1", NU), ("go0", NU), ("go1", NU)]
_swiglu_sets("F")
SETS.append(("end", 0))
ROWSUMS = 1
INDEX = {name: n + ROWSUMS for n, (name, _) in enumerate(SETS)}


def bank(name):
    return 4 * (INDEX[name] % 2)


def units_through(name):
    return sum(n for _, n in SETS[:INDEX[name] - ROWSUMS + 1])


def turned_through(name):
    return ROWSUMS + sum(n == 0 for _, n in SETS[:INDEX[name] - ROWSUMS + 1]) + (name in ("osum", "end"))


class Count:

    def __init__(self, n=0):
        self.n, self.i, self.per = n, None, 0

    def add(self, k=1):
        self.n += k
        return self.value()

    def value(self, more=0):
        return self.n + more if self.i is None else self.i * self.per + (self.n + more)


@contextmanager
def turns(eng, times, *counts):
    before = [c.n for c, _ in counts]
    with eng.Fori(0, times) as i:
        for c, per in counts:
            c.i, c.per = i, per
        yield i
    for (c, per), n in zip(counts, before):
        assert c.n == n + per, "a count grew by another amount than stated"
        c.i, c.n = None, n + per * times


def build_trunk(nc, x_T, weights, spatial_T, spatial_bias, vectors, w_g2, level_masks, identity, out_T):
    with ExitStack() as ctx:
        top = [(nc.sbuf_base + 31) // 32 * 32]

        def place(name, shape, dt=F32, over=None):
            at = top[0] if over is None else over
            words = 1
            for s in shape[1:]:
                words *= s
            if over is None:
                top[0] = at + (words * (1 if dt == U8 else 4) + 31) // 32 * 32
            t = nc.alloc_sbuf_tensor_at(name, shape, dt, offset=at)
            return t, at

        xT, _ = place("xT", [P, ND, T])
        h_hi, _ = place("h_hi", [P, ND, T], F32R)
        h_lo, _ = place("h_lo", [P, ND, T], F32R)
        y_hi, at_yhi = place("y_hi", [P, GROUP, T], F32R)
        y_lo, at_ylo = place("y_lo", [P, GROUP, T], F32R)
        raw, _ = place("raw", [P, RING, UK * UC])
        w_hi, _ = place("w_hi", [P, RING, UK * UC], F32R)
        w_lo, _ = place("w_lo", [P, RING, UK * UC], F32R)
        arena, _ = place("arena", [P, 17 * 1024])
        sumsq, _ = place("sumsq", [P, T])
        square, _ = place("square", [P, 2, T])
        rstd_row, _ = place("rstd_row", [P, T])
        ident, _ = place("ident", [P, P])
        ones, _ = place("ones", [P, P])
        masks, _ = place("masks", [P, DIAG + 1, P], U8)
        vec, _ = place("vec", [P, N_VEC])
        rstd_col, _ = place("rstd_col", [P, NW])
        eps, _ = place("eps", [P, 1])
        stats, _ = place("stats", [P, NW, 6, 6])
        moments, _ = place("moments", [P, NW, 2])
        ln_rstd, _ = place("ln_rstd", [P, NW])
        rstd_o, _ = place("rstd_o", [P, NH * NW])
        glast, _ = place("glast", [P, NH, NW])
        state, _ = place("state", [P, NH, NW - 1, DV], over=at_yhi)
        v_gla, _ = place("v_gla", [P, NW, D], over=at_ylo)
        ps = ctx.enter_context(nc.psum_tensor("ps", [P, 8, T], F32))

        def region(at, a, b):
            return arena[:, at * 1024:at * 1024 + a * b].rearrange("p (a b) -> p a b", a=a)

        v_sg = region(0, NW, SGW)
        masks_in = region(0, DIAG + 1, P)
        ws_T = region(12, NG, P)
        ws_rows = region(13, NG, P)
        bias_s = region(14, NG, P)
        pair = region(15, 4, T)
        s_bias = square[:, 0, :].rearrange("p (j t) -> p j t", j=4)
        q_T = region(0, NH, T)
        k_T = region(2, NH, T)
        G_T = region(4, NH, T)
        qk_third, _ = place("qk_third", [P, NH, T], over=at_yhi)
        QK = [region(6, NH, T), region(8, NH, T), qk_third[:]]
        qG_T = G_T
        A_T = region(10, NH, T)
        gate_T = [region(12, NH, T), region(2, NH, T)]
        k_nat = region(14, NH, T)
        diag_o = region(14, NH * NW, P)
        g2_sb = arena[0:RANK, 16 * 1024:16 * 1024 + NH * DK]
        gz_T = arena[0:RANK, 16 * 1024 + T:17 * 1024]
        o_T = QK[0:2]
        o_sq = [q_T, G_T]
        result = region(0, ND, T)
        diag_x = region(14, NW, P)

        def sem(name):
            return ctx.enter_context(nc.semaphore(name))

        landed = [sem(f"weights_landed_{i}") for i in range(RING)]
        hi_ready = sem("hi_ready")
        lo_ready = sem("lo_ready")
        units_used = sem("units_used")
        turned = sem("turned")
        banks_free = sem("banks_free")
        x_landed = [sem(f"x_landed_{i}") for i in range(NU)]
        spatial_landed = sem("spatial_landed")
        eps_ready = sem("eps_ready")
        vec_landed = sem("vec_landed")
        late_landed = sem("late_landed")
        g2_landed = sem("g2_landed")
        consts_ready = sem("consts_ready")
        x_ready = sem("x_ready")
        hhi_ready = sem("hhi_ready")
        hlo_ready = sem("hlo_ready")
        sq_ready = sem("sq_ready")
        sum_ready = sem("sum_ready")
        norm_sums = sem("norm_sums")
        root_ready = sem("root_ready")
        rstd_ready = sem("rstd_ready")
        dve_own = sem("dve_own")
        act_own = sem("act_own")
        pre_ready = sem("pre_ready")
        fn_ready = sem("fn_ready")
        y_ready = sem("y_ready")
        yhi_ready = sem("yhi_ready")
        ylo_ready = sem("ylo_ready")
        v_ready = sem("v_ready")
        stats_ready = sem("stats_ready")
        var_ready = sem("var_ready")
        std_ready = sem("std_ready")
        vhat_ready = sem("vhat_ready")
        softplus_ready = sem("softplus_ready")
        diff_ready = sem("diff_ready")
        exp_ready = sem("exp_ready")
        qk_ready = sem("qk_ready")
        glast_ready = sem("glast_ready")
        o_bank_done = sem("o_bank_done")
        o_ready = sem("o_ready")
        osq_ready = sem("osq_ready")
        osq_added = sem("osq_added")
        ocopy_ready = sem("ocopy_ready")
        oroot_ready = sem("oroot_ready")
        diag_ready = sem("diag_ready")
        x_final = sem("x_final")
        gained = sem("gained")
        spread = sem("spread")
        out_ready = sem("out_ready")
        out_stored = sem("out_stored")

        block = ctx.enter_context(nc.Block())

        @block.sync
        def _(sp):
            sp.dma_start(vec[:], vectors).then_inc(vec_landed, 16)
            for k in range(NU):
                sp.dma_start(xT[:, UK * k:UK * k + UK, :], x_T[:, UK * k:UK * k + UK, :]).then_inc(x_landed[k], 16)
                sp.dma_start(raw[:, k, :], weights[k]).then_inc(landed[k], 16)
            issued = Count(RING)
            with turns(sp, UNITS // RING - 1, (issued, RING)) as i:
                for slot in range(RING):
                    sp.wait_ge(lo_ready, issued.value(1 - RING))
                    sp.dma_start(raw[:, slot, :], weights[bass.ds(i * RING + (RING + slot), 1), :, :].rearrange(
                        "u p c -> p (u c)")).then_inc(landed[slot], 16)
                    issued.add()
            for w in range(NW):
                c = slice(w * P, (w + 1) * P)
                for half in range(2):
                    sp.wait_ge(out_ready, 2 * w + half + 1)
                    sp.dma_start(out_T[half * UC:(half + 1) * UC, c].rearrange("(k p) t -> p k t", p=P),
                                 result[:, 4 * half:4 * half + 4, c]).then_inc(out_stored, 16)
            sp.wait_ge(out_stored, 32 * NW)

        @block.gpsimd
        def _(pool):
            nc.gpsimd.memset(ones[:], 1.0).then_inc(consts_ready, 1)
            pool.wait_ge(consts_ready, 1)
            nc.gpsimd.memset(ws_T[CH:P, :, 0:CH], 0.0).then_inc(consts_ready, 1)
            pool.wait_ge(consts_ready, 2)
            for n in range(5 * ND - 1):
                if n == 4:
                    pool.dma_start(bias_s, spatial_bias.partition_broadcast(P)).then_inc(late_landed, 16)
                    pool.dma_start(masks_in, level_masks).then_inc(late_landed, 16)
                    pool.dma_start(ident[:], identity).then_inc(late_landed, 16)
                if n == ND:
                    pool.wait_ge(late_landed, 48)
                    nc.gpsimd.tensor_copy(masks[:], masks_in).then_inc(consts_ready, 1)
                pool.wait_ge(sq_ready, n + 1)
                if n % ND == 0:
                    nc.gpsimd.tensor_copy(sumsq[:], square[:, 0, :]).then_inc(sum_ready, 1)
                else:
                    pool.wait_ge(sum_ready, n)
                    nc.gpsimd.tensor_tensor(sumsq[:], sumsq[:], square[:, n % 2, :], ALU.add).then_inc(sum_ready, 1)

        @block.tensor
        def _(pe):
            used = Count()
            sets = Count()
            y_seen = Count()
            norms = Count()
            h_before = Count()

            def open_set(wait=True):
                b = 4 * (sets.n % 2)
                if wait and (sets.i is not None or sets.n >= 2):
                    pe.wait_ge(banks_free, sets.value(-1))
                sets.add()
                return b

            def three_passes(acc, w_h, w_l, o_h, o_l, weights_stationary, start, stop):
                if weights_stationary:
                    nc.tensor.matmul(acc, w_h, o_l, start=start, stop=False)
                    nc.tensor.matmul(acc, w_h, o_h, start=False, stop=False)
                    return nc.tensor.matmul(acc, w_l, o_h, start=False, stop=stop)
                nc.tensor.matmul(acc, o_h, w_l, start=start, stop=False)
                nc.tensor.matmul(acc, o_h, w_h, start=False, stop=False)
                return nc.tensor.matmul(acc, o_l, w_h, start=False, stop=stop)

            def norm_matmuls(b):
                pe.wait_ge(sum_ready, norms.add() * ND)
                nc.tensor.matmul(ps[:, b + 3, :], ones[:], sumsq[:], start=True, stop=True)
                for w in range(NW):
                    m = nc.tensor.matmul(ps[:, b + 2, w:w + 1], sumsq[:, w * P:(w + 1) * P], ones[:, 0:1],
                                         start=True, stop=True)
                m.then_inc(norm_sums, 1)

            def product_set(hi, lo, nk, natural=False, tiles=range(4), wait_h=False, wait_y=False,
                            norm_inside=False, norm_before=False, in_second=None, in_third=None, bank_free=None):
                b = open_set(wait=bank_free is None)
                for k in range(0, nk, UK):
                    pe.wait_ge(lo_ready, used.value(1))
                    if wait_h:
                        pe.wait_ge(hlo_ready, h_before.n + k + UK)
                    if wait_y:
                        pe.wait_ge(ylo_ready, y_seen.value(k + UK))
                    slot = used.n % RING
                    for t in tiles:
                        if bank_free is not None and k == 0:
                            bank_free(t)
                        if in_second is not None and k == UK:
                            in_second(t)
                        if in_third is not None and k == 2 * UK and t == 1:
                            in_third()
                        if norm_before and k == 0 and t == 2:
                            pe.wait_ge(root_ready, norms.n)
                        if norm_inside and k == nk - UK and t == 0:
                            pe.wait_ge(banks_free, sets.n - 1)
                            norm_matmuls(4 - b)
                        for j in range(UK):
                            start, stop = k + j == 0, k + j == nk - 1
                            if natural:
                                c, o = slice(j * UC, (j + 1) * UC), slice(t * P, (t + 1) * P)
                            else:
                                c, o = slice(j * UC + t * P, j * UC + (t + 1) * P), slice(0, T)
                            m = three_passes(ps[:, b + t, :], w_hi[:, slot, c], w_lo[:, slot, c],
                                             hi[:, k + j, o], lo[:, k + j, o], not natural, start, stop)
                    m.then_inc(units_used, 1)
                    used.add()

            def in_set(**kw):
                product_set(h_hi, h_lo, ND, **kw)

            def out_sets(nk):
                for _ in range(2):
                    product_set(y_hi, y_lo, nk, wait_y=True)
                y_seen.add(nk)

            b = open_set()
            pe.wait_ge(spatial_landed, 32)
            pe.wait_ge(consts_ready, 2)
            for n in range(2):
                m = nc.tensor.matmul(ps[:, b + n, :], ones[:], ws_T[:, 4 * n:4 * n + 4, :], start=True, stop=True)
            m.then_inc(turned, 1)

            in_set(natural=True, wait_h=True, norm_inside=True)
            in_set(natural=True, norm_before=True)
            with turns(pe, 2, (used, 2 * NU), (sets, 2)):
                in_set(natural=True)
                in_set(natural=True)
            for g in range(NC_SG // GROUP):
                for s in range(2):
                    in_set()
                    b = open_set()
                    pe.wait_ge(vhat_ready, NW)
                    for j in range(4):
                        c = g * GROUP + 4 * s + j
                        for w in range(NW):
                            m = nc.tensor.matmul(ps[:, b + j, w * P:(w + 1) * P], v_sg[:, w, c * P:(c + 1) * P],
                                                 ws_T[:, c // CT_G, :], start=True, stop=True)
                    m.then_inc(turned, 1)
                out_sets(GROUP)

            def swiglu(last=False):
                h_before.add(ND)
                in_set(wait_h=True, norm_inside=True)
                with turns(pe, 2, (used, TURN_UNITS), (sets, TURN_SETS), (y_seen, GROUP)):
                    in_set(norm_before=True)
                    in_set()
                    in_set()
                    out_sets(GROUP)
                    in_set()
                in_set()
                in_set()
                if not last:
                    out_sets(LAST)
                    return
                product_set(y_hi, y_lo, LAST, wait_y=True)
                b = open_set()
                pe.wait_ge(lo_ready, used.value(LAST // UK))
                for t in range(4):
                    for k in range(LAST):
                        slot, j = (used.n + k // UK) % RING, k % UK
                        c = slice(j * UC + t * P, j * UC + (t + 1) * P)
                        m = three_passes(ps[:, b + t, :], w_hi[:, slot, c], w_lo[:, slot, c], y_hi[:, k, :],
                                         y_lo[:, k, :], True, k == 0, k == LAST - 1)
                    m.then_inc(x_final, 1)
                used.add(LAST // UK)

            swiglu()

            h_before.add(ND)
            in_set(wait_h=True, norm_inside=True)
            in_set(tiles=(GZ_TILE,))
            z_bank = open_set()

            def gate_logits(tile):
                if tile > 0:
                    return
                pe.wait_ge(g2_landed, 16)
                for h in range(NH):
                    m = nc.tensor.matmul(ps[:, z_bank + h, :], g2_sb[:, h * P:(h + 1) * P], gz_T, start=True,
                                         stop=True)
                m.then_inc(turned, 1)

            def gz_taken(t):
                if t == GZ_TILE:
                    pe.wait_ge(banks_free, INDEX["gz"] + 1)

            in_set(norm_before=True, in_second=gate_logits, bank_free=gz_taken)

            def level(item):
                b = open_set()
                pe.wait_ge(qk_ready, item + 1)
                qk = QK[item % 3]
                for h in range(NH):
                    for w in range(NW):
                        c = slice(w * P, (w + 1) * P)
                        late = qk[:, h, c].rearrange("p (n s) -> p n s", s=2 * ITEMS[item])[:, :, ITEMS[item]:]
                        m = nc.tensor.matmul(ps[:, b + h, w * P:w * P + P // 2], qk[:, h, c], late,
                                             start=True, stop=True)
                m.then_inc(turned, 1)

            in_set(natural=True)
            level(0)
            level(1)
            level(2)
            in_set(natural=True)
            level(3)
            b = open_set()
            pe.wait_ge(qk_ready, END + 1)
            pe.wait_ge(late_landed, 48)
            for h in range(NH):
                for w in range(NW - 1):
                    c = slice(w * P, (w + 1) * P)
                    m = nc.tensor.transpose(ps[:, b + h, c], QK[END % 3][:, h, c], ident[:])
            m.then_inc(turned, 1)
            b = open_set()
            for h in range(NH):
                for w in range(NW):
                    c = slice(w * P, (w + 1) * P)
                    m = nc.tensor.matmul(ps[:, b + h, c], k_T[:, h, c], q_T[:, h, c], start=True, stop=True)
            m.then_inc(turned, 1)

            def state_updates(windows):
                b = open_set()
                pe.wait_ge(banks_free, INDEX["KT"] + 1)
                pe.wait_ge(v_ready, 8 * NW)
                for h in range(NH):
                    for n, w in enumerate(windows):
                        m = nc.tensor.matmul(ps[:, b + h, n * DV:(n + 1) * DV], k_nat[:, h, w * P:(w + 1) * P],
                                             v_gla[:, w, h * DV:(h + 1) * DV], start=True, stop=True)
                m.then_inc(turned, 1)

            state_updates((0, 1))
            level(4)
            state_updates((2,))
            in_set()
            level(6)
            level(7)
            for part in range(2):
                b = open_set()
                pe.wait_ge(banks_free, INDEX["KV1"] + 1)
                pe.wait_ge(qk_ready, 9)
                for j in range(4):
                    h, v0 = 2 * part + j // 2, j % 2 * P
                    for w in range(1, NW):
                        c = slice(w * P, (w + 1) * P)
                        nc.tensor.matmul(ps[:, b + j, c], state[:, h, w - 1, v0:v0 + P], qG_T[:, h, c],
                                         start=w == 1, stop=False)
                pe.wait_ge(banks_free, INDEX["L6"] + 1)
                for j in range(4):
                    h, v0 = 2 * part + j // 2, j % 2 * P
                    for w in range(NW):
                        c = slice(w * P, (w + 1) * P)
                        m = nc.tensor.matmul(ps[:, b + j, c], v_gla[:, w, h * DV + v0:h * DV + v0 + P], A_T[:, h, c],
                                             start=False, stop=w == NW - 1)
                    m.then_inc(o_bank_done if j < 3 else turned, 1)
            o_bank = open_set()

            def head_sums(h):
                if h == 0:
                    pe.wait_ge(osq_added, 2)
                for w in range(NW):
                    n = h * NW + w
                    m = nc.tensor.matmul(ps[:, o_bank + 3, n:n + 1], o_sq[h // 2][:, 2 * (h % 2), w * P:(w + 1) * P],
                                         ones[:, 0:1], start=True, stop=True)
                if h == NH - 1:
                    m.then_inc(turned, 1)

            def spread_rstd():
                pe.wait_ge(diag_ready, 1)
                for h in range(NH):
                    for w in range(NW):
                        m = nc.tensor.matmul(ps[:, o_bank + h, w * P:(w + 1) * P], ones[:],
                                             diag_o[:, h * NW + w, :], start=True, stop=True)
                m.then_inc(turned, 1)

            def o_taken(t):
                pe.wait_ge((o_ready, ocopy_ready)[t % 2], 2 + t // 2 + 1)

            in_set(in_second=head_sums, in_third=spread_rstd, bank_free=o_taken)
            out_sets(ND)

            swiglu(last=True)
            b = open_set()
            pe.wait_ge(sum_ready, 5 * ND - 1)
            for w in range(NW):
                nc.tensor.matmul(ps[:, b + 2, w:w + 1], sumsq[:, w * P:(w + 1) * P], ones[:, 0:1],
                                 start=w == 0, stop=False)
            pe.wait_ge(sq_ready, 5 * ND)
            for w in range(NW):
                m = nc.tensor.matmul(ps[:, b + 2, w:w + 1], square[:, (ND - 1) % 2, w * P:(w + 1) * P],
                                     ones[:, 0:1], start=False, stop=w == NW - 1)
            m.then_inc(norm_sums, 1)
            for w in range(NW):
                pe.wait_ge(diag_ready, w + 2)
                nc.tensor.matmul(ps[:, b + w, 0:P], ones[:], diag_x[:, w, :],
                                 start=True, stop=True).then_inc(spread, 1)

        @block.scalar
        def _(act):
            unit = Count()
            x_seen, pre, y_seen, norms, squares, diffs = (Count() for _ in range(6))

            def split():
                if unit.i is None and unit.n >= UNITS:
                    return
                slot, rounds = unit.n % RING, 16 * (unit.n // RING + 1)
                act.wait_ge(landed[slot], rounds if unit.i is None else unit.i * (16 * unit.per // RING) + rounds)
                if unit.i is not None or unit.n >= RING:
                    act.wait_ge(units_used, unit.value(1 - RING))
                nc.scalar.copy(w_hi[:, slot, :], raw[:, slot, :]).then_inc(hi_ready, 1)
                unit.add()

            def drain(n, piece=None):
                if piece is not None:
                    for j in range(4):
                        piece(j)
                for _ in range(n):
                    split()

            def finish_norm(b):
                act.wait_ge(norm_sums, norms.add())
                nc.scalar.activation(rstd_col[:], ps[:, b + 2, 0:NW], ACT.Sqrt, bias=eps[:, 0:1], scale=1.0 / D)
                nc.scalar.activation(rstd_row[:], ps[:, b + 3, :], ACT.Sqrt, bias=eps[:, 0:1],
                                     scale=1.0 / D).then_inc(root_ready, 1)

            def square_tile(tile):
                if squares.n > 1:
                    act.wait_ge(sum_ready, squares.n - 1)
                nc.scalar.activation(square[:, squares.n % 2, :], xT[:, tile, :], ACT.Square).then_inc(sq_ready, 1)
                squares.add()

            def upper_h(tile, gain):
                nc.scalar.activation(h_hi[:, tile, :], xT[:, tile, :], ACT.Copy,
                                     scale=vec[:, GAIN + gain * ND + tile:GAIN + gain * ND + tile + 1]).then_inc(
                                         hhi_ready, 1)

            def drain_out(n, gain):
                for half in range(2):
                    def piece(j):
                        if gain is None:
                            x_seen.add()
                            return
                        act.wait_ge(x_ready, x_seen.add())
                        if gain == FINAL:
                            tile = 4 * half + j
                            square_tile(tile)
                            nc.scalar.activation(result[:, tile, :], xT[:, tile, :], ACT.Copy,
                                                 scale=vec[:, GAIN + gain * ND + tile:GAIN + gain * ND + tile + 1]
                                                 ).then_inc(gained, 1)
                        else:
                            upper_h(4 * half + j, gain)
                            square_tile(4 * half + j)
                    drain(n, piece)

            def upper_y(tile, source):
                act.wait_ge(y_ready, y_seen.add())
                nc.scalar.copy(y_hi[:, tile, :], source).then_inc(yhi_ready, 1)

            def function(tile, f):
                act.wait_ge(pre_ready, pre.add())
                nc.scalar.activation(tile, tile, f).then_inc(fn_ready, 1)

            act.dma_start(ws_T[0:CH], spatial_T[0:CH]).then_inc(spatial_landed, 16)
            act.dma_start(ws_T[CH:P, :, CH:P], spatial_T[CH:P, :, CH:P]).then_inc(spatial_landed, 16)
            act.wait_ge(consts_ready, 1)
            nc.scalar.activation(eps[:], ones[:, 0:1], ACT.Copy, scale=EPS).then_inc(eps_ready, 1)
            act.wait_ge(vec_landed, 16)
            for tile in range(ND):
                if tile % UK == 0:
                    act.wait_ge(x_landed[tile // UK], 16)
                upper_h(tile, MIX0)
                if tile % UK == 1:
                    split()
                    square_tile(tile - 1)
                    square_tile(tile)
            drain(LEAD - ND // 2)

            act.wait_ge(eps_ready, 1)
            finish_norm(bank("v1"))
            act.wait_ge(rstd_ready, norms.n)
            act.wait_ge(consts_ready, 3)

            def v_set(s, col):
                split()
                for w in range(NW):
                    nc.scalar.activation(v_sg[:, w, bass.ds(col, UC)], ps[:, bank(f"v{s}") + w, :], ACT.Gelu,
                                         scale=rstd_col[:, w:w + 1]).then_inc(v_ready, 1)

            with turns(act, 2, (unit, 2 * NU)) as i:
                for s in range(2):
                    v_set(s, i * (2 * UC) + s * UC)
                    drain(NU - 1)
            v_set(4, 4 * UC)
            drain(NU - 1)
            v_set(5, 5 * UC)
            act.wait_ge(var_ready, 1)
            nc.scalar.activation(ln_rstd[:], moments[:, :, 1], ACT.Sqrt, bias=eps[:, 0:1]).then_inc(std_ready, 1)
            drain(NU - 1)

            for g in range(NC_SG // GROUP):
                for s in range(2):
                    for j in range(4):
                        function(pair[:, j, :], ACT.Gelu)
                    split()
                    for j in range(4):
                        upper_y(4 * s + j, pair[:, j, :])
                    drain(NU - 1)
                drain_out(GROUP // UK, FFN0 if g == 2 else None)

            def gate_up(tile0):
                for j in range(2):
                    function(pair[:, j, :], ACT.Silu)
                split()
                for j in range(2):
                    upper_y(tile0 + j, pair[:, j, :])
                drain(NU - 1)

            def swiglu(f, gain):
                finish_norm(bank(f + "g1"))
                gate_up(0)
                with turns(act, 2, (unit, TURN_UNITS), (pre, GROUP), (y_seen, GROUP), (x_seen, ND)):
                    for s in range(1, 4):
                        gate_up(2 * s)
                    drain_out(GROUP // UK, None)
                    gate_up(0)
                for s in range(1, 3):
                    gate_up(2 * s)
                drain_out(LAST // UK, gain)

            swiglu("f", MIX1)

            act.wait_ge(ylo_ready, y_seen.n)
            act.dma_start(g2_sb, w_g2).then_inc(g2_landed, 16)
            finish_norm(bank("gz"))
            drain(NU)
            drain(1)
            act.wait_ge(banks_free, INDEX["z"] + 1)
            nc.scalar.activation(QK[0], G_T, ACT.Abs).then_inc(act_own, 1)
            act.wait_ge(act_own, 1)
            nc.scalar.activation(QK[0], QK[0], ACT.Exp, scale=-1.0).then_inc(act_own, 1)
            act.wait_ge(act_own, 2)
            nc.scalar.activation(QK[0], QK[0], ACT.Ln, bias=ones[:, 0:1]).then_inc(softplus_ready, 1)
            drain(NU - 1)

            def exponential():
                buf = QK[diffs.n % 3]
                act.wait_ge(diff_ready, diffs.add())
                nc.scalar.activation(buf, buf, ACT.Exp, scale=1.0 / TAU).then_inc(exp_ready, 1)

            exponential()
            exponential()
            split()
            exponential()
            nc.scalar.activation(glast[:], G_T[:, :, P - 1::P], ACT.Exp, scale=1.0 / TAU).then_inc(glast_ready, 1)
            drain(NU - 1)

            def v_pieces(half):
                name = f"gv{half}"
                act.wait_ge(units_used, units_through(name))
                for w in range(NW):
                    nc.scalar.activation(v_gla[:, w, half * UC:(half + 1) * UC], ps[:, bank(name) + w, :], ACT.Copy,
                                         scale=rstd_col[:, w:w + 1]).then_inc(v_ready, 1)
                split()

            v_pieces(0)
            for _ in range(3):
                exponential()
            drain(NU - 1)
            v_pieces(1)
            for _ in range(2):
                exponential()
            act.wait_ge(diff_ready, 8)
            act.wait_ge(glast_ready, 1)
            nc.scalar.activation(G_T, G_T, ACT.Exp, scale=1.0 / TAU).then_inc(exp_ready, 1)
            drain(NU - 1)
            drain(1, lambda j: function(gate_T[0][:, j, :], ACT.Silu))
            for part in range(2):
                for j in (1, 3):
                    if j == 1:
                        act.wait_ge(o_bank_done, 3 * part + j + 1)
                    else:
                        act.wait_ge(turned, turned_through(f"o{part}"))
                    nc.scalar.copy(o_T[part][:, j, :], ps[:, bank(f"o{part}") + j, :]).then_inc(ocopy_ready, 1)
                act.wait_ge(ocopy_ready, 2 * part + 2)
                act.wait_ge(o_ready, 2 * part + 2)
                for j in range(4):
                    nc.scalar.activation(o_sq[part][:, j, :], o_T[part][:, j, :], ACT.Square).then_inc(osq_ready, 1)
            act.wait_ge(turned, turned_through("osum") - 1)
            nc.scalar.activation(rstd_o[:], ps[:, bank("osum") + 3, 0:NH * NW], ACT.Sqrt, bias=eps[:, 0:1],
                                 scale=1.0 / DV).then_inc(oroot_ready, 1)
            for t in range(4):
                upper_y(t, o_T[0][:, t, :])
            drain(NU - 1)
            for j in range(4):
                function(gate_T[1][:, j, :], ACT.Silu)
            for t in range(4):
                upper_y(4 + t, o_T[1][:, t, :])
            drain(NU)
            drain_out(NU, FFN1)

            swiglu("F", FINAL)
            act.wait_ge(norm_sums, norms.add())
            nc.scalar.activation(rstd_col[:], ps[:, bank("end") + 2, 0:NW], ACT.Sqrt, bias=eps[:, 0:1],
                                 scale=1.0 / D).then_inc(root_ready, 1)

        @block.vector
        def _(dve):
            unit = Count()
            drained = Count()
            sets = Count()
            x_done, h_done, pre, y_done, norms, v_seen, own, y_made = (Count() for _ in range(8))

            def split():
                if unit.i is None and unit.n >= UNITS:
                    return
                slot = unit.n % RING
                dve.wait_ge(hi_ready, unit.value(1))
                nc.vector.tensor_tensor(w_lo[:, slot, :], raw[:, slot, :], w_hi[:, slot, :].bitcast(F32),
                                        ALU.subtract).then_inc(lo_ready, 1)
                unit.add()

            def splits(n):
                for _ in range(n):
                    split()

            def product_banks(n):
                b = 4 * (sets.n % 2)
                dve.wait_ge(units_used, drained.add(n))
                sets.add()
                return b

            def turned_banks(name):
                b = 4 * (sets.n % 2)
                assert sets.i is not None or sets.n == INDEX[name]
                dve.wait_ge(turned, turned_through(name))
                sets.add()
                return b

            def after_own(ins):
                ins.then_inc(dve_own, 1)
                dve.wait_ge(dve_own, own.add())

            def finish_norm():
                dve.wait_ge(root_ready, norms.add())
                nc.vector.reciprocal(rstd_col[:], rstd_col[:])
                nc.vector.reciprocal(rstd_row[:], rstd_row[:]).then_inc(rstd_ready, 1)
                dve.wait_ge(rstd_ready, norms.n)

            def lower_h(tile, gain):
                dve.wait_ge(hhi_ready, h_done.add())
                nc.vector.scalar_tensor_tensor(out=h_lo[:, tile, :], in0=xT[:, tile, :],
                                               scalar=vec[:, GAIN + gain * ND + tile:GAIN + gain * ND + tile + 1],
                                               in1=h_hi[:, tile, :].bitcast(F32), op0=ALU.mult,
                                               op1=ALU.subtract).then_inc(hlo_ready, 1)

            def drain_out(n, gain):
                for half in range(2):
                    very_last = gain == FINAL and half == 1
                    if very_last:
                        b = 4 * (sets.n % 2)
                    else:
                        b = product_banks(n)
                    for j in range(4):
                        tile = 4 * half + j
                        if very_last:
                            dve.wait_ge(x_final, j + 1)
                        nc.vector.tensor_tensor(xT[:, tile, :], ps[:, b + j, :], xT[:, tile, :], ALU.add).then_inc(
                            x_ready, 1)
                        x_done.add()
                        if gain not in (None, FINAL) and j > 0:
                            lower_h(tile - 1, gain)
                    if very_last:
                        return
                    dve.wait_ge(x_ready, x_done.value())
                    dve.sem_inc(banks_free, 1)
                    if gain not in (None, FINAL):
                        lower_h(4 * half + 3, gain)
                    splits(n)

            def lower_y(tile, source):
                dve.wait_ge(yhi_ready, y_done.add())
                nc.vector.tensor_tensor(y_lo[:, tile, :], source, y_hi[:, tile, :].bitcast(F32),
                                        ALU.subtract).then_inc(ylo_ready, 1)

            dve.wait_ge(vec_landed, 16)
            for tile in range(ND):
                if tile % UK == 0:
                    dve.wait_ge(x_landed[tile // UK], 16)
                lower_h(tile, MIX0)
                if tile % 2:
                    split()
            b = 4 * (sets.n % 2)
            dve.wait_ge(turned, 1)
            nc.vector.tensor_copy(ws_rows.rearrange("p g t -> p (g t)"),
                                  ps[:, b:b + 2, :].rearrange("p a t -> p (a t)")).then_inc(banks_free, 1)
            sets.add()
            splits(LEAD - ND // 2)

            finish_norm()

            def v_set(n):
                dve.wait_ge(v_ready, v_seen.add(NW))
                split()
                for w in range(NW):
                    nc.vector.bn_stats(stats[:, w, bass.ds(n, 1), :].rearrange("p a s -> p (a s)"),
                                       v_sg[:, w, bass.ds(n * UC, UC)]).then_inc(stats_ready, 1)
                dve.sem_inc(banks_free, 1)
                drained.add(NU)
                sets.add()

            with turns(dve, 2, (unit, 2 * NU), (drained, 2 * NU), (sets, 2), (v_seen, 2 * NW)) as i:
                for s in range(2):
                    v_set(i * 2 + s)
                    splits(NU - 1)
            v_set(4)
            splits(NU - 1)
            v_set(5)
            dve.wait_ge(stats_ready, 6 * NW)
            for w in range(NW):
                m = nc.vector.bn_aggr(moments[:, w, :], stats[:, w, :, :].rearrange("p a s -> p (a s)"))
            m.then_inc(var_ready, 1)
            dve.wait_ge(std_ready, 1)
            after_own(nc.vector.reciprocal(ln_rstd[:], ln_rstd[:]))
            for w in range(NW):
                nc.vector.tensor_scalar(v_sg[:, w, :], v_sg[:, w, :], moments[:, w, 0:1], ln_rstd[:, w:w + 1],
                                        ALU.subtract, ALU.mult).then_inc(vhat_ready, 1)
            splits(NU - 1)

            dve.wait_ge(late_landed, 48)
            for g in range(NC_SG // GROUP):
                for s in range(2):
                    b = product_banks(NU)
                    if y_done.n:
                        dve.wait_ge(ylo_ready, y_done.n)
                    for j in range(4):
                        nc.vector.tensor_tensor(pair[:, j, :], ps[:, b + j, :], rstd_row[:], ALU.mult).then_inc(
                            pre_ready, 1)
                        pre.add()
                    dve.wait_ge(pre_ready, pre.n)
                    dve.sem_inc(banks_free, 1)
                    split()
                    for j in range(4):
                        c = g * GROUP + 4 * s + j
                        m = nc.vector.scalar_tensor_tensor(
                            out=s_bias[:, j, :], in0=ws_rows[:, c // CT_G, :], scalar=vec[:, LN_B + c:LN_B + c + 1],
                            in1=bias_s[:, c // CT_G, :], op0=ALU.mult, op1=ALU.add)
                    after_own(m)
                    dve.wait_ge(fn_ready, pre.n)
                    b = turned_banks(f"s{g}{s}")
                    for j in range(4):
                        c = g * GROUP + 4 * s + j
                        acc = ps[:, b + j, :].rearrange("p (w t) -> p w t", w=NW)
                        m = nc.vector.scalar_tensor_tensor(
                            out=acc, in0=acc, scalar=vec[:, LN_G + c:LN_G + c + 1],
                            in1=s_bias[:, j:j + 1, :].broadcast_to([P, NW, P]), op0=ALU.mult, op1=ALU.add)
                    after_own(m)
                    for j in range(4):
                        nc.vector.tensor_tensor(pair[:, j, :], ps[:, b + j, :], pair[:, j, :], ALU.mult).then_inc(
                            y_ready, 1)
                        y_made.add()
                    dve.wait_ge(y_ready, y_made.n)
                    dve.sem_inc(banks_free, 1)
                    for j in range(4):
                        lower_y(4 * s + j, pair[:, j, :])
                    splits(NU - 1)
                drain_out(GROUP // UK, FFN0 if g == 2 else None)

            def gate_up(tile0):
                def scale(j):
                    nc.vector.tensor_tensor(pair[:, 2 + j, :], ps[:, b + 2 + j, :], rstd_row[:], ALU.mult)
                    nc.vector.tensor_tensor(pair[:, j, :], ps[:, b + j, :], rstd_row[:], ALU.mult).then_inc(
                        pre_ready, 1)
                    pre.add()

                def multiply(j):
                    dve.wait_ge(fn_ready, pre.value(j - 1))
                    nc.vector.tensor_tensor(pair[:, j, :], pair[:, j, :], pair[:, 2 + j, :], ALU.mult).then_inc(
                        y_ready, 1)

                b = product_banks(NU)
                dve.wait_ge(ylo_ready, y_done.value())
                scale(0)
                scale(1)
                multiply(0)
                multiply(1)
                dve.sem_inc(banks_free, 1)
                split()
                lower_y(tile0, pair[:, 0, :])
                lower_y(tile0 + 1, pair[:, 1, :])
                splits(NU - 1)

            def swiglu(gain):
                finish_norm()
                gate_up(0)
                with turns(dve, 2, (unit, TURN_UNITS), (drained, TURN_UNITS), (sets, TURN_SETS),
                           (pre, GROUP), (y_done, GROUP), (x_done, ND)):
                    for s in range(1, 4):
                        gate_up(2 * s)
                    drain_out(GROUP // UK, None)
                    gate_up(0)
                for s in range(1, 3):
                    gate_up(2 * s)
                drain_out(LAST // UK, gain)

            swiglu(MIX1)

            finish_norm()
            b = product_banks(NU)
            for h in range(NH):
                m = nc.vector.scalar_tensor_tensor(out=q_T[:, h, :], in0=ps[:, b + h, :], scalar=float(DK) ** -0.5,
                                                   in1=rstd_row[:], op0=ALU.mult, op1=ALU.mult)
            m.then_inc(banks_free, 1)
            splits(2)
            b = product_banks(NU)
            dve.wait_ge(g2_landed, 16)
            nc.vector.tensor_tensor(gz_T, ps[0:RANK, b + GZ_TILE, :], rstd_row[0:RANK, :], ALU.mult).then_inc(banks_free, 1)
            splits(NU - 1)
            b = turned_banks("z")
            for h in range(NH):
                m = nc.vector.tensor_scalar(G_T[:, h, :], ps[:, b + h, :], vec[:, GATE_B + h:GATE_B + h + 1], None,
                                            ALU.add)
            m.then_inc(banks_free, 1)
            after_own(nc.vector.memset(A_T, 0.0))
            dve.wait_ge(softplus_ready, 1)
            after_own(nc.vector.scalar_tensor_tensor(out=QK[1], in0=G_T, scalar=0.0, in1=QK[0], op0=ALU.min,
                                                     op1=ALU.subtract))
            splits(NU - 1)
            for h in range(NH):
                for w in range(NW):
                    c = slice(w * P, (w + 1) * P)
                    m = nc.vector.tensor_tensor_scan(G_T[:, h, c], ones[:], QK[1][:, h, c], 0.0, ALU.mult, ALU.add)
            after_own(m)

            def halves(x, m):
                v = x.rearrange("p h (n s) -> p (h n) s", s=2 * m)
                return v[:, :, 0:m], v[:, :, m:2 * m]

            def differences(item):
                buf = QK[item % 3]
                kind = ITEMS[item]
                if kind == "end":
                    g = G_T.rearrange("p h (n s) -> p (h n) s", s=P)
                    nc.vector.tensor_tensor(buf.rearrange("p h (n s) -> p (h n) s", s=P),
                                            g[:, :, P - 1:P].broadcast_to([P, NH * NW, P]), g,
                                            ALU.subtract).then_inc(diff_ready, 1)
                else:
                    g_early, g_late = halves(G_T, kind)
                    early, late = halves(buf, kind)
                    middle = g_early[:, :, kind - 1:kind].broadcast_to([P, NH * T // (2 * kind), kind])
                    nc.vector.tensor_tensor(late, g_late, middle, ALU.subtract)
                    nc.vector.tensor_tensor(early, middle, g_early, ALU.subtract).then_inc(diff_ready, 1)

            def decayed(item):
                buf = QK[item % 3]
                kind = ITEMS[item]
                dve.wait_ge(exp_ready, item + 1)
                if kind == "end":
                    nc.vector.tensor_tensor(buf, buf, k_T, ALU.mult).then_inc(qk_ready, 1)
                else:
                    early, late = halves(buf, kind)
                    nc.vector.tensor_tensor(late, late, halves(q_T, kind)[1], ALU.mult)
                    nc.vector.tensor_tensor(early, early, halves(k_T, kind)[0], ALU.mult).then_inc(qk_ready, 1)

            def take_level(name, mask):
                dve.wait_ge(banks_free, INDEX[name])
                b = turned_banks(name)
                attn = A_T.rearrange("p h (w t) -> p (h w) t", t=P)
                acc = ps[:, b:b + NH, :].rearrange("p h (w t) -> p (h w) t", t=P)
                keep = masks[:, mask:mask + 1, :]
                if mask != DIAG:
                    m = LEVELS[mask]
                    attn = attn.rearrange("p w (n s) -> p w n s", s=2 * m)[:, :, :, m:]
                    acc = acc[:, :, 0:P // 2].rearrange("p w (n s) -> p w n s", s=m)
                    keep = keep.rearrange("p w (n s) -> p w n s", s=2 * m)[:, :, :, m:]
                    keep = keep.broadcast_to([P, NH * NW, P // (2 * m), m])
                else:
                    keep = keep.broadcast_to([P, NH * NW, P])
                nc.vector.copy_predicated(attn, keep, acc).then_inc(banks_free, 1)

            def gate(part):
                b = product_banks(NU)
                for j in range(4):
                    nc.vector.tensor_tensor(gate_T[part][:, j, :], ps[:, b + j, :], rstd_row[:], ALU.mult).then_inc(
                        pre_ready, 1)
                    pre.add()
                dve.wait_ge(pre_ready, pre.n)
                dve.sem_inc(banks_free, 1)

            def pass_v(half):
                product_banks(NU)
                dve.wait_ge(v_ready, (6 + half + 1) * NW)
                dve.sem_inc(banks_free, 1)

            for item in range(3):
                differences(item)
            b = product_banks(NU)
            for h in range(NH):
                m = nc.vector.tensor_tensor(k_T[:, h, :], ps[:, b + h, :], rstd_row[:], ALU.mult)
            m.then_inc(banks_free, 1)
            dve.wait_ge(banks_free, INDEX["k"] + 1)
            split()
            decayed(0)
            decayed(1)
            decayed(2)
            splits(NU - 1)
            pass_v(0)
            take_level("L0", 0)
            differences(3)
            take_level("L1", 1)
            differences(4)
            take_level("L2", 2)
            differences(5)
            decayed(3)
            decayed(4)
            split()
            decayed(5)
            splits(NU - 1)
            pass_v(1)
            take_level("L3", 3)
            b = turned_banks("KT")
            nc.vector.tensor_copy(k_nat[:, :, 0:(NW - 1) * P], ps[:, b:b + NH, 0:(NW - 1) * P]).then_inc(banks_free, 1)
            differences(6)
            take_level("Ld", DIAG)
            b = turned_banks("KV0")
            after_own(nc.vector.tensor_copy(state[:, :, 0, :], ps[:, b:b + NH, 0:DV]))
            dve.wait_ge(glast_ready, 1)
            for h in range(NH):
                m = nc.vector.scalar_tensor_tensor(out=state[:, h, 1, :], in0=state[:, h, 0, :],
                                                   scalar=glast[:, h, 1:2], in1=ps[:, b + h, DV:2 * DV],
                                                   op0=ALU.mult, op1=ALU.add)
            m.then_inc(banks_free, 1)
            take_level("L4", 4)
            b = turned_banks("KV1")
            for h in range(NH):
                m = nc.vector.scalar_tensor_tensor(out=state[:, h, 2, :], in0=state[:, h, 1, :],
                                                   scalar=glast[:, h, 2:3], in1=ps[:, b + h, 0:DV],
                                                   op0=ALU.mult, op1=ALU.add)
            m.then_inc(banks_free, 1)
            differences(7)
            split()
            decayed(6)
            decayed(7)
            dve.wait_ge(exp_ready, 9)
            nc.vector.tensor_tensor(qG_T, G_T, q_T, ALU.mult).then_inc(qk_ready, 1)
            splits(NU - 1)
            gate(0)
            split()
            take_level("L5", 5)
            take_level("L6", 6)
            for part in range(2):
                b = bank(f"o{part}")
                sets.add()
                for j in (0, 2):
                    dve.wait_ge(o_bank_done, 3 * part + j + 1)
                    nc.vector.tensor_copy(o_T[part][:, j, :], ps[:, b + j, :]).then_inc(o_ready, 1)
                dve.wait_ge(o_ready, 2 * part + 2)
                dve.wait_ge(ocopy_ready, 2 * part + 2)
                dve.sem_inc(banks_free, 1)
                dve.wait_ge(osq_ready, 4 * part + 4)
                squares = o_sq[part].rearrange("p (h a) t -> p h a t", a=2)
                nc.vector.tensor_tensor(squares[:, :, 0, :], squares[:, :, 0, :], squares[:, :, 1, :],
                                        ALU.add).then_inc(osq_added, 1)

            def gated(t):
                o = o_T[t // 4][:, t % 4, :]
                return nc.vector.scalar_tensor_tensor(out=o, in0=o, scalar=vec[:, GN_G + t:GN_G + t + 1],
                                                      in1=gate_T[t // 4][:, t % 4, :], op0=ALU.mult, op1=ALU.mult)

            dve.wait_ge(oroot_ready, 1)
            after_own(nc.vector.reciprocal(rstd_o[:], rstd_o[:]))
            nc.vector.tensor_tensor(diag_o, ident[:].rearrange("p (n t) -> p n t", n=1).broadcast_to([P, NH * NW, P]),
                                    rstd_o[:].rearrange("p (n t) -> p n t", t=1).broadcast_to([P, NH * NW, P]),
                                    ALU.mult).then_inc(diag_ready, 1)
            for t in range(4):
                m = gated(t)
            after_own(m)
            b = turned_banks("osum")
            for t in range(ND):
                o = o_T[t // 4][:, t % 4, :]
                m = nc.vector.tensor_tensor(o, ps[:, b + t // 2, :], o, ALU.mult)
                if t < 4:
                    m.then_inc(y_ready, 1)
            after_own(m)
            dve.sem_inc(banks_free, 1)
            for t in range(4):
                lower_y(t, o_T[0][:, t, :])
            splits(NU - 1)
            gate(1)
            dve.wait_ge(fn_ready, pre.n)
            for t in range(4, ND):
                gated(t).then_inc(y_ready, 1)
            for t in range(4, ND):
                lower_y(t, o_T[1][:, t - 4, :])
            splits(NU)
            drain_out(NU, FFN1)

            swiglu(FINAL)
            dve.wait_ge(root_ready, norms.add())
            after_own(nc.vector.reciprocal(rstd_col[:], rstd_col[:]))
            for w in range(NW):
                nc.vector.tensor_scalar(diag_x[:, w, :], ident[:], rstd_col[:, w:w + 1], None,
                                        ALU.mult).then_inc(diag_ready, 1)
            b = bank("end")
            dve.wait_ge(gained, ND)
            for w in range(NW):
                c = slice(w * P, (w + 1) * P)
                dve.wait_ge(spread, w + 1)
                for half in range(2):
                    piece = result[:, 4 * half:4 * half + 4, c]
                    nc.vector.tensor_tensor(piece, ps[:, b + w:b + w + 1, 0:P].broadcast_to([P, 4, P]), piece,
                                            ALU.mult).then_inc(out_ready, 1)


def _weight_stream(np, a_w_in, a_w_out, b_w_in, b_w_out, gate, up, down):
    units = []

    def one(w, col, k0=0, nk=None):
        nk = w.shape[0] // P if nk is None else nk
        for k in range(k0, k0 + nk, UK):
            units.append(w[k * P:(k + UK) * P, col:col + UC].reshape(UK, P, UC).transpose(1, 0, 2))

    def swiglu(g, u, d):
        for s in range(11):
            for k in range(0, ND, UK):
                both = [w[k * P:(k + UK) * P, s * 256:(s + 1) * 256].reshape(UK, P, 256) for w in (g, u)]
                units.append(np.concatenate(both, axis=2).transpose(1, 0, 2))
            if s in (3, 7):
                for half in range(2):
                    one(d, half * UC, (s - 3) * 2, GROUP)
        for half in range(2):
            one(d, half * UC, 2 * GROUP, LAST)

    for s in range(6):
        one(a_w_in, SGW + s * UC)
    for g in range(NC_SG // GROUP):
        one(a_w_in, 2 * g * UC)
        one(a_w_in, (2 * g + 1) * UC)
        for half in range(2):
            one(a_w_out, half * UC, g * GROUP, GROUP)
    swiglu(gate[0], up[0], down[0])
    low_rank = np.zeros((D, UC), b_w_in.dtype)
    low_rank[:, GZ_TILE * P:GZ_TILE * P + RANK] = b_w_in[:, 6 * UC:6 * UC + RANK]
    one(b_w_in, 0)
    one(low_rank, 0)
    for s in (1, 2, 3, 4, 5):
        one(b_w_in, s * UC)
    for half in range(2):
        one(b_w_out, half * UC)
    swiglu(gate[1], up[1], down[1])
    assert len(units) == UNITS
    return np.stack(units).reshape(UNITS, P, UK * UC)


def kernel(**inputs):
    import numpy as np
    import concourse.bacc as bacc
    from concourse.bass_utils import run_bass_kernel_spmd

    a = {n: np.asarray(v) for n, v in inputs.items()}
    columns = [np.stack([a["mix_norm"][0], a["ffn_norm"][0], a["mix_norm"][1], a["ffn_norm"][1],
                         a["final_norm"]]).reshape(5 * ND, P),
               a["a_ln_g"].reshape(-1, P), a["a_ln_b"].reshape(-1, P), a["b_b_g"].reshape(-1, P),
               a["b_gn_g"].reshape(-1, P)]
    at = np.arange(P)
    key, query = at[:, None], at[None, :]
    level_masks = [(key // (2 * m) == query // (2 * m)) & (key % (2 * m) < m) & (query % (2 * m) >= m)
                   for m in LEVELS] + [key == query]
    arrays = {
        "x_T": a["x"][0].T.reshape(ND, P, T).transpose(1, 0, 2),
        "weights": _weight_stream(np, a["a_w_in"][0], a["a_w_out"][0], a["b_w_in"][0], a["b_w_out"][0],
                                  a["ffn_w_gate"], a["ffn_w_up"], a["ffn_w_down"]),
        "spatial_T": a["a_w_s"][0].transpose(2, 0, 1),
        "spatial_bias": a["a_b_s"][0],
        "vectors": np.concatenate(columns).T,
        "w_g2": a["b_w_g2"][0],
        "level_masks": np.stack(level_masks, axis=1).astype(np.float32),
        "identity": np.eye(P, dtype=np.float32),
    }
    arrays = {n: np.ascontiguousarray(v) for n, v in arrays.items()}
    nc = bacc.Bacc("TRN2", target_bir_lowering=False, num_devices=1)
    args = {n: nc.dram_tensor(n, v.shape, mybir.dt.from_np(v.dtype), kind="ExternalInput").ap()
            for n, v in arrays.items()}
    out_T = nc.dram_tensor("out_T", (D, T), F32, kind="ExternalOutput").ap()
    build_trunk(nc, out_T=out_T, **args)
    run = run_bass_kernel_spmd(nc, [arrays], core_ids=[0])
    return np.ascontiguousarray(run.results[0]["out_T"].T)[None]
```
